# Optimizing a Trainium2 kernel written in Bass

```python
import math
import jax, jax.numpy as jnp
from jax import lax
import numpy as np

D_MODEL = 1024
BATCH = 1
SEQ = 512
DEPTH = 2

N_A_LAYERS = DEPTH // 2
N_B_LAYERS = DEPTH - N_A_LAYERS
CONV_WIDTH = 31
N_HEADS = 16
HEAD_DIM = D_MODEL // N_HEADS
D_FF = 4 * D_MODEL
D_PLE = 256
Q_BLOCK = 128
EPS = 1e-6
NEG_BIG = -1e30


def rmsnorm(x, g):
    xf = x.astype(jnp.float32)
    y = xf * lax.rsqrt(jnp.mean(xf * xf, axis=-1, keepdims=True) + EPS)
    return (y * g.astype(jnp.float32)).astype(x.dtype)

def layernorm(x, g, b):
    xf = x.astype(jnp.float32)
    mu = jnp.mean(xf, axis=-1, keepdims=True)
    xc = xf - mu
    var = jnp.mean(xc * xc, axis=-1, keepdims=True)
    y = xc * lax.rsqrt(var + EPS)
    return (y * g.astype(jnp.float32) + b.astype(jnp.float32)).astype(x.dtype)

def conformer_conv(hn, w_pw1, b_pw1, w_dw, b_dw, ln_g, ln_b, w_pw2, b_pw2):
    u = hn @ w_pw1 + b_pw1
    a, g = jnp.split(u, 2, axis=-1)
    u = a * jax.nn.sigmoid(g)
    kern = w_dw[:, None, :].astype(u.dtype)
    u = lax.conv_general_dilated(
        u, kern, window_strides=(1,), padding=((CONV_WIDTH - 1, 0),),
        dimension_numbers=("NWC", "WIO", "NWC"),
        feature_group_count=D_MODEL) + b_dw
    u = layernorm(u, ln_g, ln_b)
    u = jax.nn.silu(u)
    return u @ w_pw2 + b_pw2

def shared_kv(h, kv_norm, w_kvf, b_f):
    B, S, _ = h.shape
    u = rmsnorm(h, kv_norm) @ w_kvf
    k = u[..., :D_MODEL].reshape(B, S, N_HEADS, HEAD_DIM)
    v = u[..., D_MODEL:2 * D_MODEL].reshape(B, S, N_HEADS, HEAD_DIM)
    f_logit = (u[..., 2 * D_MODEL:] + b_f).astype(jnp.float32)
    log_f = jax.nn.log_sigmoid(f_logit)
    c = jnp.cumsum(log_f, axis=1)
    return k, v, jnp.transpose(c, (0, 2, 1))

def fox_attention(hn, w_q, w_o, k, v, c_bhs):
    B, S, _ = hn.shape
    nb = S // Q_BLOCK
    q = (hn @ w_q).reshape(B, S, N_HEADS, HEAD_DIM) * (HEAD_DIM ** -0.5)
    qb = jnp.transpose(q.reshape(B, nb, Q_BLOCK, N_HEADS, HEAD_DIM), (1, 0, 2, 3, 4))
    cb = jnp.transpose(c_bhs.reshape(B, N_HEADS, nb, Q_BLOCK), (2, 0, 1, 3))
    k_pos = jnp.arange(S)

    def one_block(args):
        q_blk, c_blk, i = args
        s = jnp.einsum("bqhd,bkhd->bhqk", q_blk, k,
                       preferred_element_type=jnp.float32)
        bias = c_blk[:, :, :, None] - c_bhs[:, :, None, :]
        q_pos = i * Q_BLOCK + jnp.arange(Q_BLOCK)
        causal = k_pos[None, :] <= q_pos[:, None]
        s = jnp.where(causal, s + bias, NEG_BIG)
        pr = jax.nn.softmax(s, axis=-1)
        return jnp.einsum("bhqk,bkhd->bqhd", pr.astype(v.dtype), v)

    o = lax.map(one_block, (qb, cb, jnp.arange(nb)))
    o = jnp.transpose(o, (1, 0, 2, 3, 4)).reshape(B, S, D_MODEL)
    return o @ w_o

def first_inputs(seed: int = 0) -> dict:
    key = jax.random.key(seed)
    ks = jax.random.split(key, 32)
    f32 = jnp.float32
    nrm = lambda k, shape, scale: (jax.random.normal(k, shape, f32) * scale)
    gain = lambda k, shape: 1.0 + 0.05 * jax.random.normal(k, shape, f32)
    D = D_MODEL
    x = jax.random.normal(ks[0], (BATCH, SEQ, D), f32)
    p = jax.random.normal(ks[1], (DEPTH, BATCH, SEQ, D_PLE), f32)
    mix_norm = gain(ks[2], (DEPTH, D))
    conv_w_pw1 = nrm(ks[3], (N_A_LAYERS, D, 2 * D), D ** -0.5)
    conv_b_pw1 = nrm(ks[4], (N_A_LAYERS, 2 * D), 0.02)
    conv_w_dw = nrm(ks[5], (N_A_LAYERS, CONV_WIDTH, D), CONV_WIDTH ** -0.5)
    conv_b_dw = nrm(ks[6], (N_A_LAYERS, D), 0.02)
    conv_ln_g = gain(ks[7], (N_A_LAYERS, D))
    conv_ln_b = nrm(ks[8], (N_A_LAYERS, D), 0.02)
    conv_w_pw2 = nrm(ks[9], (N_A_LAYERS, D, D), 0.5 * D ** -0.5)
    conv_b_pw2 = nrm(ks[10], (N_A_LAYERS, D), 0.02)
    kv_norm = gain(ks[11], (D,))
    w_kvf = jnp.concatenate([
        nrm(ks[12], (D, 2 * D), D ** -0.5),
        nrm(ks[13], (D, N_HEADS), 0.1 * D ** -0.5),
    ], axis=1)
    b_f = jax.random.uniform(ks[14], (N_HEADS,), f32, 1.0, 6.0)
    attn_w_q = nrm(ks[15], (N_B_LAYERS, D, D), D ** -0.5)
    attn_w_o = nrm(ks[16], (N_B_LAYERS, D, D), 0.5 * D ** -0.5)
    ffn_norm = gain(ks[17], (DEPTH, D))
    ffn_w1 = nrm(ks[18], (DEPTH, D, D_FF), D ** -0.5)
    ffn_w2 = nrm(ks[19], (DEPTH, D_FF, D), 0.5 * D_FF ** -0.5)
    ple_norm = gain(ks[20], (DEPTH, D))
    ple_w_gate = nrm(ks[21], (DEPTH, D, D), D ** -0.5)
    ple_w_proj = nrm(ks[22], (DEPTH, D_PLE, D), 0.5 * D_PLE ** -0.5)
    final_norm = gain(ks[23], (D,))
    return {"x": x, "p": p, "mix_norm": mix_norm,
            "conv_w_pw1": conv_w_pw1, "conv_b_pw1": conv_b_pw1,
            "conv_w_dw": conv_w_dw, "conv_b_dw": conv_b_dw,
            "conv_ln_g": conv_ln_g, "conv_ln_b": conv_ln_b,
            "conv_w_pw2": conv_w_pw2, "conv_b_pw2": conv_b_pw2,
            "kv_norm": kv_norm, "w_kvf": w_kvf, "b_f": b_f,
            "attn_w_q": attn_w_q, "attn_w_o": attn_w_o,
            "ffn_norm": ffn_norm, "ffn_w1": ffn_w1, "ffn_w2": ffn_w2,
            "ple_norm": ple_norm, "ple_w_gate": ple_w_gate, "ple_w_proj": ple_w_proj,
            "final_norm": final_norm}

def first_block(x, p, mix_norm, conv_w_pw1, conv_b_pw1, conv_w_dw, conv_b_dw,
              conv_ln_g, conv_ln_b, conv_w_pw2, conv_b_pw2, kv_norm, w_kvf, b_f,
              attn_w_q, attn_w_o, ffn_norm, ffn_w1, ffn_w2, ple_norm, ple_w_gate,
              ple_w_proj, final_norm):
    h = x
    k = v = c_bhs = None
    for i in range(DEPTH):
        hn = rmsnorm(h, mix_norm[i])
        if i < N_A_LAYERS:
            h = h + conformer_conv(hn, conv_w_pw1[i], conv_b_pw1[i], conv_w_dw[i],
                                   conv_b_dw[i], conv_ln_g[i], conv_ln_b[i],
                                   conv_w_pw2[i], conv_b_pw2[i])
        else:
            j = i - N_A_LAYERS
            if j == 0:
                k, v, c_bhs = shared_kv(h, kv_norm, w_kvf, b_f)
            h = h + fox_attention(hn, attn_w_q[j], attn_w_o[j], k, v, c_bhs)
        hn = rmsnorm(h, ffn_norm[i])
        h = h + jnp.square(jax.nn.relu(hn @ ffn_w1[i])) @ ffn_w2[i]
        gate = jax.nn.sigmoid(rmsnorm(h, ple_norm[i]) @ ple_w_gate[i])
        h = h + gate * (p[i] @ ple_w_proj[i])
    return rmsnorm(h, final_norm)


DEPTH_2 = 1

LRU_WIDTH = 512
LRU_HEADS = 8
LRU_HEAD_DIM = LRU_WIDTH // LRU_HEADS
LRU_CONV = 4
LRU_C = 8.0
MOBA_HEADS = 8
MOBA_HEAD_DIM = 64
MOBA_WIDTH = MOBA_HEADS * MOBA_HEAD_DIM
MOBA_BLOCK = 256
MOBA_TOPK = 3
MOBA_Q_CHUNK = 16
MEM_LEN = 256
XATTN_HEADS = 4
XATTN_HEAD_DIM = 128
XATTN_WIDTH = XATTN_HEADS * XATTN_HEAD_DIM
N_BRANCH = 3
IN_COLS = 2 * LRU_WIDTH + 3 * MOBA_WIDTH + XATTN_WIDTH + N_BRANCH * D_MODEL
D_FF_2 = 3 * D_MODEL
FFN_CONV = 3
NORM_EPS = 1e-6


def rms_norm(x, g):
    x32 = x.astype(jnp.float32)
    y = x32 * lax.rsqrt(jnp.mean(x32 * x32, axis=-1, keepdims=True) + NORM_EPS)
    return (y * g.astype(jnp.float32)).astype(x.dtype)

def causal_dwconv(x, w, b):
    k, c = w.shape
    y = lax.conv_general_dilated(x, w[:, None, :].astype(x.dtype), (1,), [(k - 1, 0)],
                                 dimension_numbers=("NWC", "WIO", "NWC"),
                                 feature_group_count=c)
    return y + b.astype(x.dtype)

def rg_lru(x, w_a, b_a, w_x, b_x, lam):
    bsz, s, w = x.shape
    xh = x.reshape(bsz, s, LRU_HEADS, LRU_HEAD_DIM)
    r = jax.nn.sigmoid((jnp.einsum("bshi,hij->bshj", xh, w_a) + b_a).reshape(bsz, s, w).astype(jnp.float32))
    i = jax.nn.sigmoid((jnp.einsum("bshi,hij->bshj", xh, w_x) + b_x).reshape(bsz, s, w).astype(jnp.float32))
    log_a = -LRU_C * r * jax.nn.softplus(-lam.astype(jnp.float32))
    a = jnp.exp(log_a)
    mult = jnp.sqrt(-jnp.expm1(2.0 * log_a))
    u = mult * i * x.astype(jnp.float32)

    def combine(lhs, rhs):
        a1, b1 = lhs
        a2, b2 = rhs
        return a1 * a2, a2 * b1 + b2

    _, h = lax.associative_scan(combine, (a, u), axis=1)
    return h.astype(x.dtype)

def alibi_slopes(n_heads):
    return jnp.exp2(-8.0 * jnp.arange(1, n_heads + 1, dtype=jnp.float32) / n_heads)

def moba_attention(q, k, v):
    bsz, nh, s, dh = q.shape
    nb = -(-s // MOBA_BLOCK)
    sp = nb * MOBA_BLOCK
    pad = ((0, 0), (0, 0), (0, sp - s), (0, 0))
    q, k, v = jnp.pad(q, pad), jnp.pad(k, pad), jnp.pad(v, pad)
    kb = k.reshape(bsz, nh, nb, MOBA_BLOCK, dh)
    vb = v.reshape(bsz, nh, nb, MOBA_BLOCK, dh)
    kmean = jnp.mean(kb.astype(jnp.float32), axis=3)
    n_sel = min(MOBA_TOPK, nb - 1)
    slopes = alibi_slopes(nh)[None, :, None]
    scale = dh ** -0.5
    nq = sp // MOBA_Q_CHUNK
    qc = q.reshape(bsz, nh, nq, MOBA_Q_CHUNK, dh).transpose(2, 0, 1, 3, 4)
    bi = jnp.arange(bsz)[:, None, None, None]
    hi = jnp.arange(nh)[None, :, None, None]
    blk_pos = jnp.arange(MOBA_BLOCK)

    def attend_chunk(args):
        qi, c = args
        t = c * MOBA_Q_CHUNK + jnp.arange(MOBA_Q_CHUNK)
        own = (c * MOBA_Q_CHUNK) // MOBA_BLOCK
        k_own = lax.dynamic_index_in_dim(kb, own, axis=2, keepdims=False)
        v_own = lax.dynamic_index_in_dim(vb, own, axis=2, keepdims=False)
        dist_own = (t[:, None] - (own * MOBA_BLOCK + blk_pos)[None, :]).astype(jnp.float32)
        s_own = (jnp.einsum("bhqd,bhkd->bhqk", qi, k_own, preferred_element_type=jnp.float32) * scale
                 - slopes[..., None] * dist_own)
        s_own = jnp.where(dist_own >= 0, s_own, -jnp.inf)
        if n_sel == 0:
            p = jax.nn.softmax(s_own, axis=-1).astype(v.dtype)
            return jnp.einsum("bhqk,bhkd->bhqd", p, v_own)
        gate = jnp.einsum("bhqd,bhnd->bhqn", qi.astype(jnp.float32), kmean)
        gate = jnp.where(jnp.arange(nb) < own, gate, -jnp.inf)
        _, sel = lax.top_k(gate, n_sel)
        valid = sel < own
        ks = kb[bi, hi, sel]
        vs = vb[bi, hi, sel]
        kpos_sel = sel[..., None] * MOBA_BLOCK + blk_pos
        dist_sel = (t[None, None, :, None, None] - kpos_sel).astype(jnp.float32)
        s_sel = (jnp.einsum("bhqd,bhqnkd->bhqnk", qi, ks, preferred_element_type=jnp.float32) * scale
                 - slopes[..., None, None] * dist_sel)
        s_sel = jnp.where(valid[..., None], s_sel, -jnp.inf)
        nsk = n_sel * MOBA_BLOCK
        scores = jnp.concatenate([s_sel.reshape(bsz, nh, MOBA_Q_CHUNK, nsk), s_own], axis=-1)
        p = jax.nn.softmax(scores, axis=-1).astype(v.dtype)
        p_sel = p[..., :nsk].reshape(bsz, nh, MOBA_Q_CHUNK, n_sel, MOBA_BLOCK)
        p_own = p[..., nsk:]
        return (jnp.einsum("bhqnk,bhqnkd->bhqd", p_sel, vs)
                + jnp.einsum("bhqk,bhkd->bhqd", p_own, v_own))

    out = lax.map(attend_chunk, (qc, jnp.arange(nq)))
    out = out.transpose(1, 2, 0, 3, 4).reshape(bsz, nh, sp, dh)
    return out[:, :, :s]

def memory_cross_attention(q, mem_k, mem_v):
    scores = jnp.einsum("bshd,bmhd->bhsm", q, mem_k, preferred_element_type=jnp.float32) * (XATTN_HEAD_DIM ** -0.5)
    p = jax.nn.softmax(scores, axis=-1).astype(mem_v.dtype)
    o = jnp.einsum("bhsm,bmhd->bshd", p, mem_v)
    return o.reshape(q.shape[0], q.shape[1], XATTN_WIDTH)

def second_inputs(seed: int = 0) -> dict:
    key = jax.random.key(seed)
    ks = jax.random.split(key, 32)
    f32 = jnp.float32

    def nrm(k, shape, scale):
        return jax.random.normal(k, shape, f32) * scale

    def gain(k, shape):
        return 1.0 + 0.02 * jax.random.normal(k, shape, f32)

    u = jax.random.uniform(ks[8], (DEPTH_2, LRU_WIDTH), f32, 0.9, 0.999)
    sa = u ** (1.0 / LRU_C)
    lru_lambda = jnp.log(sa) - jnp.log1p(-sa)
    return {
        "x": nrm(ks[0], (BATCH, SEQ, D_MODEL), 1.0),
        "mem": nrm(ks[1], (BATCH, MEM_LEN, D_MODEL), 1.0),
        "mix_norm_gain": gain(ks[2], (DEPTH_2, D_MODEL)),
        "w_in": nrm(ks[3], (DEPTH_2, D_MODEL, IN_COLS), D_MODEL ** -0.5),
        "lru_conv_w": nrm(ks[4], (DEPTH_2, LRU_CONV, LRU_WIDTH), LRU_CONV ** -0.5),
        "lru_conv_b": nrm(ks[5], (DEPTH_2, LRU_WIDTH), 0.02),
        "lru_w_a": nrm(ks[6], (DEPTH_2, LRU_HEADS, LRU_HEAD_DIM, LRU_HEAD_DIM), LRU_HEAD_DIM ** -0.5),
        "lru_b_a": nrm(ks[7], (DEPTH_2, LRU_HEADS, LRU_HEAD_DIM), 0.02),
        "lru_w_x": nrm(ks[9], (DEPTH_2, LRU_HEADS, LRU_HEAD_DIM, LRU_HEAD_DIM), LRU_HEAD_DIM ** -0.5),
        "lru_b_x": nrm(ks[10], (DEPTH_2, LRU_HEADS, LRU_HEAD_DIM), 0.02),
        "lru_lambda": lru_lambda,
        "mem_norm_gain": gain(ks[11], (DEPTH_2, D_MODEL)),
        "w_mem_kv": nrm(ks[12], (DEPTH_2, D_MODEL, 2 * XATTN_WIDTH), D_MODEL ** -0.5),
        "w_branch": nrm(ks[13], (DEPTH_2, N_BRANCH, LRU_WIDTH, D_MODEL), LRU_WIDTH ** -0.5),
        "w_out": nrm(ks[14], (DEPTH_2, D_MODEL, D_MODEL), D_MODEL ** -0.5),
        "ffn_norm_gain": gain(ks[15], (DEPTH_2, D_MODEL)),
        "w_ffn_gate": nrm(ks[16], (DEPTH_2, D_MODEL, D_FF_2), D_MODEL ** -0.5),
        "w_ffn_up": nrm(ks[17], (DEPTH_2, D_MODEL, D_FF_2), D_MODEL ** -0.5),
        "ffn_conv_w": nrm(ks[18], (DEPTH_2, FFN_CONV, D_FF_2), FFN_CONV ** -0.5),
        "ffn_conv_b": nrm(ks[19], (DEPTH_2, D_FF_2), 0.02),
        "w_ffn_down": nrm(ks[20], (DEPTH_2, D_FF_2, D_MODEL), D_FF_2 ** -0.5),
        "final_norm_gain": gain(ks[21], (D_MODEL,)),
    }

def second_block(x, mem, mix_norm_gain, w_in, lru_conv_w, lru_conv_b, lru_w_a, lru_b_a, lru_w_x, lru_b_x,
              lru_lambda, mem_norm_gain, w_mem_kv, w_branch, w_out, ffn_norm_gain, w_ffn_gate, w_ffn_up,
              ffn_conv_w, ffn_conv_b, w_ffn_down, final_norm_gain):
    bsz, s, d = x.shape
    m = mem.shape[1]
    splits = list(np.cumsum([LRU_WIDTH, LRU_WIDTH, MOBA_WIDTH, MOBA_WIDTH, MOBA_WIDTH, XATTN_WIDTH]))
    for l in range(DEPTH_2):
        h = rms_norm(x, mix_norm_gain[l])
        proj = h @ w_in[l]
        xa, ga, qm, km, vm, qx, g_logits = jnp.split(proj, splits, axis=-1)
        xa = causal_dwconv(xa, lru_conv_w[l], lru_conv_b[l])
        y_a = rg_lru(xa, lru_w_a[l], lru_b_a[l], lru_w_x[l], lru_b_x[l], lru_lambda[l]) * jax.nn.gelu(ga)
        to_heads = lambda t_: t_.reshape(bsz, s, MOBA_HEADS, MOBA_HEAD_DIM).transpose(0, 2, 1, 3)
        y_b = moba_attention(to_heads(qm), to_heads(km), to_heads(vm))
        y_b = y_b.transpose(0, 2, 1, 3).reshape(bsz, s, MOBA_WIDTH)
        mkv = rms_norm(mem, mem_norm_gain[l]) @ w_mem_kv[l]
        mk, mv = jnp.split(mkv.reshape(bsz, m, 2, XATTN_HEADS, XATTN_HEAD_DIM), 2, axis=2)
        y_c = memory_cross_attention(qx.reshape(bsz, s, XATTN_HEADS, XATTN_HEAD_DIM), mk[:, :, 0], mv[:, :, 0])
        ys = jnp.stack([y_a, y_b, y_c], axis=2)
        branch_out = jnp.einsum("bsnw,nwd->bsnd", ys, w_branch[l])
        gates = jax.nn.sigmoid(g_logits.astype(jnp.float32)).astype(x.dtype).reshape(bsz, s, N_BRANCH, d)
        merged = jnp.sum(gates * branch_out, axis=2)
        x = x + merged @ w_out[l]
        h = rms_norm(x, ffn_norm_gain[l])
        g = causal_dwconv(h @ w_ffn_gate[l], ffn_conv_w[l], ffn_conv_b[l])
        x = x + (jax.nn.gelu(g) * (h @ w_ffn_up[l])) @ w_ffn_down[l]
    return rms_norm(x, final_norm_gain)


def setup_inputs(seed=0):
    out = dict(first_inputs(seed))
    for name, value in second_inputs(seed + 1).items():
        if name != "x":
            out[name + "_2"] = value
    return out


def reference(
    x, p, mix_norm, conv_w_pw1, conv_b_pw1, conv_w_dw, conv_b_dw, conv_ln_g, conv_ln_b,
    conv_w_pw2, conv_b_pw2, kv_norm, w_kvf, b_f, attn_w_q, attn_w_o, ffn_norm, ffn_w1, ffn_w2,
    ple_norm, ple_w_gate, ple_w_proj, final_norm, mem_2, mix_norm_gain_2, w_in_2, lru_conv_w_2,
    lru_conv_b_2, lru_w_a_2, lru_b_a_2, lru_w_x_2, lru_b_x_2, lru_lambda_2, mem_norm_gain_2,
    w_mem_kv_2, w_branch_2, w_out_2, ffn_norm_gain_2, w_ffn_gate_2, w_ffn_up_2, ffn_conv_w_2,
    ffn_conv_b_2, w_ffn_down_2, final_norm_gain_2,
):
    x = first_block(
        x, p, mix_norm, conv_w_pw1, conv_b_pw1, conv_w_dw, conv_b_dw, conv_ln_g, conv_ln_b,
        conv_w_pw2, conv_b_pw2, kv_norm, w_kvf, b_f, attn_w_q, attn_w_o, ffn_norm, ffn_w1,
        ffn_w2, ple_norm, ple_w_gate, ple_w_proj, final_norm,
    )
    return second_block(
        x, mem_2, mix_norm_gain_2, w_in_2, lru_conv_w_2, lru_conv_b_2, lru_w_a_2, lru_b_a_2,
        lru_w_x_2, lru_b_x_2, lru_lambda_2, mem_norm_gain_2, w_mem_kv_2, w_branch_2, w_out_2,
        ffn_norm_gain_2, w_ffn_gate_2, w_ffn_up_2, ffn_conv_w_2, ffn_conv_b_2, w_ffn_down_2,
        final_norm_gain_2,
    )


_drawn_inputs = setup_inputs


def setup_inputs(seed=0):
    import zlib

    import numpy as np

    out = dict(_drawn_inputs(seed))
    spreads = {}
    factors = {'mix_norm': 2.74,
     'conv_b_pw1': 5.219,
     'conv_b_dw': 2.767,
     'conv_ln_b': 5.596,
     'kv_norm': 4.45,
     'ple_norm': 8.0,
     'mix_norm_gain_2': 3.655,
     'lru_b_a_2': 29.157,
     'lru_b_x_2': 8.0,
     'mem_norm_gain_2': 8.0,
     'ffn_norm_gain_2': 10.471,
     'ffn_conv_b_2': 29.439,
     'final_norm_gain_2': 22.872,
     'lru_conv_b_2': 3.156}
    for name, (base, spread) in spreads.items():
        noise = np.random.default_rng([zlib.crc32(name.encode()), seed]).standard_normal(out[name].shape)
        drawn = base * np.exp(spread * noise) if base else spread * noise
        out[name] = __import__('jax').numpy.asarray(drawn.astype(out[name].dtype))
    for name, factor in factors.items():
        out[name] = (out[name] * factor).astype(out[name].dtype)
    return out
```

```python
from contextlib import ExitStack

import concourse.bass as bass
from concourse import mybir

F32 = mybir.dt.float32
F32R = mybir.dt.float32r
BF16 = mybir.dt.bfloat16
ALU = mybir.AluOpType
ACT = mybir.ActivationFunctionType
AX = mybir.AxisListType

P = 128
S = 512
D = 1024
KB = D // P
QB = S // P
SLAB = 16 * P
TAPS = 31
POOL_TAPS = 10
EPS = 1e-6
MEM = 256
HALF = 512
NEG = -1e30
ATANH = [1.0 / (2 * k + 1) for k in range(1, 9)]

PARAM_BLOCKS = [
    ("mix0", 8), ("mix1", 8), ("b_a1", 8), ("b_g1", 8), ("w_dw", 8 * TAPS), ("b_dw", 8), ("ln_g", 8), ("ln_b", 8),
    ("b_pw2", 8), ("kv", 8), ("ffn0", 8), ("ffn1", 8), ("ple0", 8), ("ple1", 8), ("final1", 8),
    ("mix2", 8), ("lru_w", 16), ("lru_b", 4), ("lru_ba", 4), ("lru_bx", 4), ("lam", 4), ("memg", 8),
    ("ffn2", 8), ("cw", 24 * 3), ("cb", 24), ("final2", 8), ("slope", 8), ("b_f", 1),
]
COL, _n = {}, 0
for _name, _k in PARAM_BLOCKS:
    COL[_name] = _n
    _n += _k
NPARAM = _n


class Pos:

    def __init__(self, const, step=0, i=0):
        self.const, self.step, self.i = const, step, i

    def at(self, d=0):
        return self.const + d + self.step * self.i

    def slot(self, ring, d=0):
        return (self.const + d) % ring

    def turns(self, ring, d=0):
        assert self.step % ring == 0
        return (self.const + d) // ring + (self.step // ring) * self.i

    def plus(self, d):
        return Pos(self.const + d, self.step, self.i)


class Ledger:

    def __init__(self):
        self.count = {}

    def take(self, name, n):
        base = self.count.get(name, 0)
        self.count[name] = base + n
        return base


def build(nc, hbm, out, upto=None):
    led = Ledger()

    def phase(slabs=0, blks=0, **more):
        at = {"slab": led.take("slab", slabs), "blk": led.take("blk", blks)}
        at.update({k: led.take(k, n) for k, n in more.items()})
        return at

    x0 = phase(split=8, sq=8, acc=7, norm=1, stat=1)
    p_split = [None, None]
    pw1 = phase(slabs=8, blks=16, sg=8)
    memkv = phase(slabs=4, blks=8)
    ln = phase(split=8, norm=1)
    pw2 = phase(slabs=4, blks=8, split=8, sq=8, acc=7, norm=1, stat=1)
    ffn, proj, gate = [None, None], [None, None], [None, None]

    def plan_ffn(l):
        ffn[l] = phase(slabs=32, blks=64, full=32, split=40, sq=8, acc=7, norm=1, stat=1)
        proj[l] = phase(slabs=1, blks=8)
        gate[l] = phase(slabs=4, blks=8, sg=8, gm=8, hg=8, split=8 if l == 0 else 0, sq=8, acc=7, norm=1, stat=1)

    plan_ffn(0)
    kvsplit = phase(split=8)
    gq = phase(slabs=4, blks=8)
    gk = phase(slabs=4, blks=8)
    gv = phase(slabs=4, blks=16)
    fox = phase(split=8, step=64, unit=8)
    wo = phase(slabs=4, blks=8, split=8, sq=8, acc=7, norm=1, stat=1)
    p_split[1] = phase(split=1)
    plan_ffn(1)
    fin = phase(split=8, sq=8, acc=7, norm=1, stat=1)
    gqx = phase(slabs=2, blks=4)
    xat = phase(split=4, step=16, unit=4)
    br = [None] * 3
    br[2] = phase(slabs=6, blks=16, sg=8)
    gxg = phase(slabs=4, blks=8)
    lru = phase(split=4)
    gqm = phase(slabs=2, blks=4)
    gkm = phase(slabs=2, blks=4)
    gvm = phase(slabs=2, blks=8)
    br[0] = phase(slabs=6, blks=16, sg=8, gm=8)
    mob = phase(split=4, step=32, unit=4)
    br[1] = phase(slabs=6, blks=16, sg=8, gm=8)
    mrg = phase(split=8)
    wout = phase(slabs=4, blks=8, split=8, sq=8, acc=7, norm=1, stat=1)
    ffn2 = phase(slabs=36, blks=72, full=24, split=24, sq=8, acc=7, norm=1, stat=1)
    NS = led.count["slab"]

    with ExitStack() as ctx:
        def sb(name, shape, dt=F32, where=ctx):
            return where.enter_context(nc.sbuf_tensor(name, shape, dt))

        def sem(name):
            return ctx.enter_context(nc.semaphore(name))

        with ExitStack() as early:
            b_hi = sb("b_hi", [P, KB, S], F32R, early)
            b_lo = sb("b_lo", [P, KB, S], F32R, early)
        kT = sb("kT", [P, KB, S])
        spare_over_b = sb("spare_over_b", [P, KB, S])
        a_hi, a_lo = sb("a_hi", [P, KB, S], F32R), sb("a_lo", [P, KB, S], F32R)
        A, B = (a_hi, a_lo), (b_hi, b_lo)
        h = sb("h", [P, KB, S])
        raw = sb("raw", [P, 2, SLAB])
        w_hi, w_lo = sb("w_hi", [P, 2, SLAB], F32R), sb("w_lo", [P, 2, SLAB], F32R)
        par = sb("par", [P, NPARAM])
        inv_d = sb("inv_d", [P, P])
        ident, identb, tri = sb("ident", [P, P]), sb("identb", [P, P], BF16), sb("tri", [P, P], BF16)
        T = sb("T", [P, 4, S])
        U = sb("U", [P, 2, S])
        acc_sq, sqb = sb("acc_sq", [P, S]), sb("sqb", [P, 2, S])
        rstd, var = sb("rstd", [P, S]), sb("var", [P, S])
        mkv = sb("mkv", [P, 4 * S])
        mk = mkv[:, 0:4 * MEM].rearrange("p (c s) -> p c s", c=4)
        mv = mkv[:, 4 * MEM:].rearrange("p (t n) -> p t n", t=2)
        rcol, colv = sb("rcol", [P, QB]), sb("colv", [P, QB])
        nmax, rsum, rinv = sb("nmax", [P, 2]), sb("rsum", [P, 4]), sb("rinv", [P, 4])
        sp = sb("sp", [P, 8, 4])
        with ExitStack() as la:
            big = sb("big", [P, KB, S], F32, la)
            upad = sb("upad", [P, 2, S + TAPS - 1], F32, la)
            pool_sum = sb("pool_sum", [P, 2, S], F32, la)
            mem_raw = sb("mem_raw", [P, KB, MEM], F32, la)
            p_raw0 = sb("p_raw0", [P, 2, S], F32, la)
            p_hi0, p_lo0 = sb("p_hi0", [P, 2, S], F32R, la), sb("p_lo0", [P, 2, S], F32R, la)
        with ExitStack() as lb:
            v_s, qT = sb("v_s", [P, QB, D], F32, lb), sb("qT", [P, KB, S], F32, lb)
            with ExitStack() as lb1:
                wf = sb("wf", [P, KB, 16], F32, lb1)
                wf_hi, wf_lo = sb("wf_hi", [P, KB, P], F32R, lb1), sb("wf_lo", [P, KB, P], F32R, lb1)
            fbias = sb("fbias", [P, 2, S], F32, lb)
        with ExitStack() as lf:
            big1 = sb("big1", [P, KB, S], F32, lf)
            p_raw1 = sb("p_raw1", [P, 2, S], F32, lf)
            p_hi1, p_lo1 = sb("p_hi1", [P, 2, S], F32R, lf), sb("p_lo1", [P, 2, S], F32R, lf)
        with ExitStack() as lc:
            merged = sb("merged", [P, KB, S], F32, lc)
            with ExitStack() as c1:
                qx = sb("qx", [P, 4, S], F32, c1)
            with ExitStack() as c2:
                xap = sb("xap", [P, 4, S + 3], F32, c2)
                ga = sb("ga", [P, 4, S], F32, c2)
                xc = sb("xc", [P, 4, S], F32, c2)
                wga, wgx = sb("wga", [P, 4, P], F32, c2), sb("wgx", [P, 4, P], F32, c2)
            with ExitStack() as c3:
                qm, vm = sb("qm", [P, 4, S], F32, c3), sb("vm", [P, QB, HALF], F32, c3)
                mbias = sb("mbias", [P, 2, 7 * P], F32, c3)
                dist = sb("dist", [P, 7 * P], F32, c3)
        with ExitStack() as ld:
            gpad = sb("gpad", [P, 2, S + 2], F32, ld)
        km = mkv[:, :].rearrange("p (c s) -> p c s", c=4)
        bigs, p_raw, p_hi, p_lo = (big, big1), (p_raw0, p_raw1), (p_hi0, p_hi1), (p_lo0, p_lo1)
        prob, probT = T[:, 0:2, :], T[:, 2:4, :]
        o_sb = U[:, 0, :].rearrange("p (t n) -> p t n", t=QB)
        qs = sqb
        dt_i = mybir.dt.int32
        mem_sq = big[:, 4:8].rearrange("p a (k s) -> p (a k) s", s=MEM)
        CONV_OPS = 2 * (TAPS - POOL_TAPS + 1)

        gp = ctx.enter_context(nc.psum_tensor("gp", [P, 4, S], F32))
        ms = ctx.enter_context(nc.psum_tensor("ms", [P, 4, S], F32))

        negc_hbm = nc.dram_tensor("negc_scratch", (16, S), F32, kind="Internal").ap()

        raw_ready = [sem(f"raw_ready{i}") for i in range(2)]
        w_hi_done, w_lo_done = sem("w_hi_done"), sem("w_lo_done")
        blk_done = sem("blk_done")
        evac = [sem(f"evacuated{i}") for i in range(4)]
        hi_done, lo_done = sem("hi_done"), sem("lo_done")
        x_ready = [sem(f"x_ready{i}") for i in range(4)]
        par_ready, mem_ready = sem("par_ready"), sem("mem_ready")
        p_ready, wf_ready, wg_ready = sem("p_ready"), sem("wf_ready"), sem("wg_ready")
        const_ready, wf_zero, wg_zero, pad_zero = sem("const_ready"), sem("wf_zero"), sem("wg_zero"), sem("pad_zero")
        sq_done, acc_done, stat_done, var_done, rstd_done = (
            sem("sq_done"), sem("acc_done"), sem("stat_done"), sem("var_done"), sem("rstd_done"))
        eps_done = sem("eps_done")
        col_stat, col_eps, col_var, col_done = sem("col_stat"), sem("col_eps"), sem("col_var"), sem("col_done")
        msq_done, mstat_done, mvar_done, mrstd_done, mscaled = (
            sem("msq_done"), sem("mstat_done"), sem("mvar_done"), sem("mrstd_done"), sem("mscaled"))
        meps_done = sem("meps_done")
        mp_hi, mp_lo = sem("mem_p_hi"), sem("mem_p_lo")
        tap_done, pool_conv = sem("tap_product"), sem("pool_conv")
        full = sem("full")
        sg_done = sem("sigmoid_done")
        u_done, conv_done = sem("u_done"), sem("conv_done")
        mean_done, centred, csq_done, cvar_done, normed = (
            sem("mean_done"), sem("centred"), sem("csq_done"), sem("cvar_done"), sem("normed"))
        gm_done, hg_done, fin_done = sem("gated"), sem("h_gated"), sem("fin_done")
        f_stat, f_v, f_exp, f_stored, f_chain = (
            sem("f_stat"), sem("f_v"), sem("f_exp"), sem("f_stored"), sem("f_chain"))
        wf_split, wf_hi_done, silu_done = sem("wf_split"), sem("wf_hi_done"), sem("silu_done")
        q_zero, q_copied, bias_ready = sem("q_zero"), sem("q_copied"), [sem(f"bias_ready{i}") for i in range(2)]
        scored, biased, exped, transposed, pt_copied, pv_done, o_done, ot_done, sum_inv = (
            sem("scored"), sem("biased"), sem("exped"), sem("transposed"), sem("pt_copied"), sem("pv_done"),
            sem("o_done"), sem("ot_done"), sem("sum_inv"))
        xa_c, l_gate, l_act, l_chain, l_u, l_y = (
            sem("xa_conv"), sem("lru_gate_mm"), sem("lru_act"), sem("lru_chain"), sem("lru_u"), sem("lru_y"))
        step_open = sem("step_open")
        sp_e, sp_chain = sem("sp_exp"), sem("sp_chain")
        g_chain, gelu_done = sem("g_chain"), sem("gelu_done")
        dist_ready, mb_ready = sem("dist_ready"), sem("mb_ready")
        out_ready, stored = sem("out_ready"), sem("stored")

        def col(name, k, n=1):
            return par[:, COL[name] + k:COL[name] + k + n]

        def f32(ap):
            return ap.bitcast(F32)

        block = ctx.enter_context(nc.Block())

        @block.sync
        def _(sp_e_):
            q = sp_e_

            def slab(pos, first):
                s = pos.slot(2)
                if not first:
                    q.wait_ge(w_lo_done, pos.at(-1))
                q.dma_start(raw[:, s], hbm["w"][pos.at()] if isinstance(pos.at(), int)
                            else hbm["w"][bass.ds(pos.at(), 1)].rearrange("a p n -> p (a n)")
                            ).then_inc(raw_ready[s], 16)

            def slabs(a, b):
                while a < 2:
                    slab(Pos(a), True)
                    a += 1
                if (b - a) % 2:
                    slab(Pos(a), False)
                    a += 1
                if b > a:
                    with q.Fori(0, (b - a) // 2) as i:
                        slab(Pos(a, 2, i), False)
                        slab(Pos(a + 1, 2, i), False)

            q.dma_start(par[:], hbm["par"]).then_inc(par_ready, 16)
            for c in range(4):
                q.dma_start(h[:, 2 * c:2 * c + 2], hbm["x"][:, 2 * c:2 * c + 2]).then_inc(x_ready[c], 16)
                if c == 0:
                    slab(Pos(0), True)
            slab(Pos(1), True)
            q.dma_start(mem_raw[:], hbm["mem"]).then_inc(mem_ready, 16)
            q.dma_start(p_raw0[:], hbm["p"][0]).then_inc(p_ready, 16)
            slabs(2, gk["slab"])
            q.wait_ge(hg_done, gate[0]["hg"] + 8)
            q.dma_start(wf[:], hbm["wf"]).then_inc(wf_ready, 16)
            slabs(gk["slab"], gv["slab"] + 2)
            q.wait_ge(f_v, 3)
            q.dma_start(negc_hbm, T[0:16, 3]).then_inc(f_stored, 16)
            q.wait_ge(f_stored, 16)

            def fox_bias(j, hh, first):
                if not first:
                    q.wait_ge(biased, 8 * j - 8 + 4 * (hh + 1))
                q.dma_start(fbias[:, hh], negc_row(2 * j + hh)).then_inc(bias_ready[hh], 16)

            def negc_row(r):
                src = negc_hbm[bass.ds(r, 1), :] if not isinstance(r, int) else negc_hbm[r:r + 1, :]
                return src.broadcast_to([P, S])
            fox_bias(0, 0, True)
            fox_bias(0, 1, True)
            slabs(gv["slab"] + 2, wo["slab"] + 2)
            with q.Fori(1, 8) as j:
                fox_bias(j, 0, False)
                fox_bias(j, 1, False)
            q.wait_ge(lo_done, fox["split"] + 8)
            q.dma_start(p_raw1[:], hbm["p"][1]).then_inc(p_ready, 16)
            slabs(wo["slab"] + 2, gxg["slab"])
            for t, name in ((wga, "w_a"), (wgx, "w_x")):
                q.wait_ge(wg_zero, 2)
                for hh in range(2):
                    q.dma_start(t[64 * hh:64 * hh + 64, :, 64 * hh:64 * hh + 64],
                                hbm[name][:, hh].rearrange("j i o -> i j o")).then_inc(wg_ready, 16)
            slabs(gxg["slab"], NS)
            o_v = out
            for c in range(4):
                q.wait_ge(out_ready, 2 * (c + 1))
                q.dma_start(o_v[:, 2 * c:2 * c + 2], h[:, 2 * c:2 * c + 2]).then_inc(stored, 16)
            q.wait_ge(stored, 64)

        @block.gpsimd
        def _(g):
            g.memset(ident[:], 0.0).then_inc(const_ready, 1)
            g.memset(identb[:], 0.0).then_inc(const_ready, 1)
            g.memset(tri[:], 0.0).then_inc(const_ready, 1)
            g.memset(inv_d[:], 1.0 / D).then_inc(const_ready, 1)
            g.memset(upad[:, :, 0:TAPS - 1], 0.0).then_inc(pad_zero, 1)
            g.wait_ge(const_ready, 4)
            for m in (ident, identb):
                g.affine_select(out=m[:], in_=m[:], compare_op=ALU.not_equal, fill=1.0, base=0,
                                pattern=[[-1, P]], channel_multiplier=1).then_inc(const_ready, 1)
            g.affine_select(out=tri[:], in_=tri[:], compare_op=ALU.is_ge, fill=NEG, base=0,
                            pattern=[[-1, P]], channel_multiplier=1).then_inc(const_ready, 1)

            def slab(pos):
                s = pos.slot(2)
                g.wait_ge(w_hi_done, pos.at(1))
                g.tensor_tensor(w_lo[:, s], raw[:, s], f32(w_hi[:, s]), ALU.subtract).then_inc(w_lo_done, 1)

            def slabs(a, b):
                if (b - a) % 2:
                    slab(Pos(a))
                    a += 1
                if b > a:
                    with g.Fori(0, (b - a) // 2) as i:
                        slab(Pos(a, 2, i))
                        slab(Pos(a + 1, 2, i))

            def copies(q_of, at, n, base, slabs_before):
                def one(j, first):
                    for hh in range(2):
                        lo, hi = 64 * hh, 64 * hh + 64
                        if not first:
                            g.wait_ge(scored, at["step"] + 8 * j - 8 + 4 * (hh + 1))
                        if not (first and hh == 0):
                            g.wait_ge(q_copied, base + 2 * j + hh)
                        g.tensor_copy(qs[lo:hi, hh], q_of(lo, hi, j)).then_inc(q_copied, 1)
                g.wait_ge(w_lo_done, slabs_before)
                g.memset(qs[:, 0], 0.0).then_inc(q_zero, 1)
                g.memset(qs[:, 1], 0.0).then_inc(q_zero, 1)
                g.wait_ge(q_zero, base // 8 + 2)
                one(0, True)
                with g.Fori(1, n) as j:
                    one(j, False)
                g.wait_ge(q_copied, base + 2 * n)

            def dyn(t):
                return lambda lo, hi, j: t[lo:hi, j, :] if isinstance(j, int) else t[lo:hi, bass.ds(j, 1), :].rearrange("p a s -> p (a s)")

            def add_taps(i):
                for t in range(1, POOL_TAPS):
                    for s in range(2):
                        g.wait_ge(tap_done, 2 * POOL_TAPS * i + 2 * t + s + 1)
                        if t >= 2:
                            g.wait_ge(pool_conv, 2 * (POOL_TAPS - 1) * i + 2 * t + s - 3)
                        g.tensor_tensor(pool_sum[:, s], pool_sum[:, s], sqb[:, s], ALU.add).then_inc(pool_conv, 1)

            slabs(0, 4)
            add_taps(0)
            g.wait_ge(mp_hi, 1)
            g.tensor_tensor(b_lo[:, :, 0:MEM], mem_raw[:], f32(b_hi[:, :, 0:MEM]), ALU.subtract).then_inc(mp_lo, 1)
            g.wait_ge(mp_hi, 2)
            g.tensor_tensor(p_lo0[:], p_raw0[:], f32(p_hi0[:]), ALU.subtract).then_inc(mp_lo, 1)
            with g.Fori(1, 4) as i:
                for s in range(2):
                    slab(Pos(2 + s, 2, i))
                add_taps(i)
            slabs(10, gq["slab"] + 1)
            g.wait_ge(hg_done, gate[0]["hg"] + 8)
            g.memset(f32(wf_hi[:]), 0.0).then_inc(wf_zero, 1)
            g.memset(f32(wf_lo[:]), 0.0).then_inc(wf_zero, 1)
            slabs(gq["slab"] + 1, wo["slab"] + 1)
            g.wait_ge(f_stored, 16)
            copies(dyn(qT), fox, 8, 0, wo["slab"] + 1)
            slabs(wo["slab"] + 1, gxg["slab"] + 0)
            g.wait_ge(lo_done, xat["split"] + 4)
            g.memset(wga[:], 0.0).then_inc(wg_zero, 1)
            g.memset(wgx[:], 0.0).then_inc(wg_zero, 1)
            g.memset(xap[:, :, 0:3], 0.0).then_inc(pad_zero, 1)
            slabs(gxg["slab"] + 0, br[1]["slab"] + 1)
            g.wait_ge(lo_done, lru["split"] + 4)
            g.iota(dist[:].bitcast(dt_i), pattern=[[1, 7 * P]], base=-3 * P, channel_multiplier=-1).then_inc(dist_ready, 1)
            g.wait_ge(dist_ready, 1)
            g.tensor_copy(dist[:], dist[:].bitcast(dt_i)).then_inc(dist_ready, 1)
            last = gvm["blk"] + 7
            g.wait_ge(evac[3], last // 4 + 1)
            copies(dyn(qm), mob, 4, 16, br[1]["slab"] + 1)
            slabs(br[1]["slab"] + 1, ffn2["slab"])
            g.wait_ge(lo_done, mrg["split"] + 8)
            g.memset(gpad[:, :, 0:2], 0.0).then_inc(pad_zero, 1)
            slabs(ffn2["slab"], NS)

        def wait_blk(eng, pos, c):
            eng.wait_ge(blk_done, pos.at(c + 1))

        def wait_evac(eng, pos, c):
            eng.wait_ge(evac[pos.slot(4, c)], pos.turns(4, c) + 1)

        @block.tensor
        def _(pe):
            def free_bank(pos, c):
                b = pos.slot(4, c)
                if pos.const + c >= 4:
                    pe.wait_ge(evac[b], pos.turns(4, c))
                return b

            def three(o, wh, wl, xh, xl, start, stop):
                pe.matmul(o, wh, xh, start=start, stop=False)
                pe.matmul(o, wh, xl, start=False, stop=False)
                return pe.matmul(o, wl, xh, start=False, stop=stop)

            def slab_ws(sp_, bp, x, k0=0, kk=8, n=S, ready=None, hook=None):
                s = sp_.slot(2)
                cc = 16 // kk
                pe.wait_ge(w_lo_done, sp_.at(1))
                for c in range(cc):
                    b = free_bank(bp, c)
                    for k in range(kk):
                        if ready is not None and c == 0:
                            pe.wait_ge(lo_done, ready.at(k + 1))
                        at = (k * cc + c) * P
                        m = three(gp[:, b, 0:n], w_hi[:, s, at:at + P], w_lo[:, s, at:at + P],
                                  x[0][:, k0 + k, 0:n], x[1][:, k0 + k, 0:n], k == 0, k == kk - 1)
                    m.then_inc(blk_done, 1)
                    if hook and c == 0:
                        hook()

            def slab_xs(sp_, bp, x, tiles):
                s = sp_.slot(2)
                pe.wait_ge(w_lo_done, sp_.at(1))
                for t in range(tiles):
                    b = free_bank(bp, t)
                    for k in range(8):
                        xh, xl = x[0][:, k, t * P:t * P + P], x[1][:, k, t * P:t * P + P]
                        wh, wl = w_hi[:, s, k * 256:k * 256 + 256], w_lo[:, s, k * 256:k * 256 + 256]
                        m = three(gp[:, b, 0:256], xh, xl, wh, wl, k == 0, k == 7)
                    m.then_inc(blk_done, 1)

            def gemm(at, x, n_slabs=4, hook=None, ready=None, off=0, boff=None, **kw):
                boff = 2 * off if boff is None else boff
                a = 0
                if hook or ready is not None:
                    for a in range(2):
                        slab_ws(Pos(at["slab"] + off + a), Pos(at["blk"] + boff + 2 * a), x,
                                ready=Pos(ready) if a == 0 else None, hook=hook if a == 0 else None, **kw)
                    a = 2
                if n_slabs > a:
                    if n_slabs - a == 2:
                        for s in range(2):
                            slab_ws(Pos(at["slab"] + off + a + s), Pos(at["blk"] + boff + 2 * (a + s)), x, **kw)
                    else:
                        with pe.Fori(0, (n_slabs - a) // 2) as i:
                            for s in range(2):
                                slab_ws(Pos(at["slab"] + off + a + s, 2, i), Pos(at["blk"] + boff + 2 * (a + s), 4, i), x, **kw)

            def stat(at, src_ready):
                pe.wait_ge(acc_done, src_ready)
                pe.matmul(ms[:, 0, :], inv_d[:], acc_sq[:], start=True, stop=True).then_inc(stat_done, 1)

            def col_stats():
                for t in range(QB):
                    m = pe.matmul(ms[:, 1, t:t + 1], acc_sq[:, t * P:t * P + P], inv_d[:, 0:1],
                                  start=True, stop=True, skip_group_check=True)
                m.then_inc(col_stat, 1)

            pe.wait_ge(const_ready, 7)
            def memory_stat():
                pe.wait_ge(msq_done, 1)
                for k in range(8):
                    m = pe.matmul(ms[:, 1, 0:MEM], inv_d[:], mem_sq[:, k], start=(k == 0), stop=(k == 7))
                m.then_inc(mstat_done, 1)
            for s in range(2):
                slab_ws(Pos(s), Pos(2 * s), A, ready=Pos(x0["split"]) if s == 0 else None,
                        hook=memory_stat if s else lambda: stat(x0, x0["acc"] + 7))
            with pe.Fori(0, 3) as i:
                for s in range(2):
                    slab_ws(Pos(2 + s, 2, i), Pos(4 + 2 * s, 4, i), A)
            pe.wait_ge(mp_lo, 1)
            for s in range(2):
                slab_ws(Pos(memkv["slab"] + s), Pos(memkv["blk"] + 2 * s), B, n=MEM)
            for k in range(8):
                pe.wait_ge(conv_done, CONV_OPS * (k // 2 + 1))
                m = pe.matmul(ms[:, 1, :], inv_d[:], big[:, k], start=(k == 0), stop=(k == 7))
            m.then_inc(mean_done, 1)
            slab_xs(Pos(memkv["slab"] + 2), Pos(memkv["blk"] + 4), B, 2)
            for k in range(8):
                pe.wait_ge(csq_done, k + 1)
                pe.matmul(ms[:, 2, :], inv_d[:], sqb[:, k % 2], start=(k == 0), stop=(k == 7)).then_inc(cvar_done, 1)
            slab_xs(Pos(memkv["slab"] + 3), Pos(memkv["blk"] + 6), B, 2)
            gemm(pw2, B, ready=ln["split"])

            def ffn_layer(l, X, H_):
                f = ffn[l]
                src = pw2 if l == 0 else wo
                gemm(f, X, ready=src["split"], hook=lambda: stat(f, src["acc"] + 7))
                with pe.Fori(0, 3) as i:
                    for s in range(8):
                        down = s < 4
                        slab_ws(Pos(f["slab"] + 4 + s, 8, i), Pos(f["blk"] + 8 + 2 * s, 16, i),
                                H_ if down else X, ready=Pos(f["split"], 8, i) if s == 0 else None)
                for s in range(4):
                    slab_ws(Pos(f["slab"] + 28 + s), Pos(f["blk"] + 56 + 2 * s), H_, ready=Pos(f["split"] + 24) if s == 0 else None)
                if l == 0:
                    pe.wait_ge(mp_lo, 2)
                else:
                    pe.wait_ge(lo_done, p_split[l]["split"] + 1)
                slab_ws(Pos(proj[l]["slab"]), Pos(proj[l]["blk"]), (p_hi[l], p_lo[l]), kk=2)
                gemm(gate[l], X, ready=f["split"] + 32, hook=lambda: stat(gate[l], f["acc"] + 7))

            ffn_layer(0, A, B)

            def kv_stats():
                stat(gq, gate[0]["acc"] + 7)
                col_stats()
            gemm(gq, B, ready=gate[0]["split"], hook=kv_stats)
            pe.wait_ge(lo_done, kvsplit["split"] + 8)
            pe.wait_ge(wf_split, 1)
            for k in range(8):
                m = three(ms[:, 2, :], wf_hi[:, k], wf_lo[:, k], a_hi[:, k], a_lo[:, k], k == 0, k == 7)
            m.then_inc(f_stat, 1)
            gemm(gk, A)
            with pe.Fori(0, 2) as i:
                for s in range(2):
                    slab_xs(Pos(gv["slab"] + s, 2, i), Pos(gv["blk"] + 4 * s, 8, i), A, 4)

            def attention(at, n, s_read, n_of, scores, v_of, vw, before_unit, looped):
                t0, per = at["step"], len(n_of)

                def T_(pos, s):
                    pe.wait_ge(exped, pos.at(s + 1))
                    if pos.const + s - t0 >= 2 or pos.step:
                        pe.wait_ge(pt_copied, pos.at(s - 1))
                    for kb in range(n_of[s % per]):
                        m = pe.transpose(ms[:, 2 + s % 2, kb * P:kb * P + P], prob[:, s % 2, kb * P:kb * P + P], ident[:])
                    m.then_inc(transposed, 1)

                def S_(pos, j, s, first):
                    if before_unit:
                        before_unit(j, s)
                    if not (first and s < 2):
                        pe.wait_ge(s_read, pos.at(s - 1))
                    scores(j, s).then_inc(scored, 1)

                def V_(pos, j, s):
                    pe.wait_ge(pt_copied, pos.at(s + 1))
                    if pos.const + s - t0 >= 2 or pos.step:
                        pe.wait_ge(o_done, pos.at(s - 1))
                    for kb in range(n_of[s % per]):
                        m = pe.matmul(gp[:, s % 2, 0:vw], probT[:, s % 2, kb * P:kb * P + P], v_of(j, s % per, kb),
                                      start=(kb == 0), stop=(kb == n_of[s % per] - 1))
                    m.then_inc(pv_done, 1)

                def O_(pos, j, up):
                    pe.wait_ge(o_done, pos.at(per))
                    if not isinstance(j, int) or j > 0:
                        pe.wait_ge(lo_done, up)
                    for t in range(QB):
                        m = pe.transpose(gp[:, 2, t * P:t * P + P], o_sb[:, t, :], ident[:])
                    m.then_inc(ot_done, 1)

                def unit(pos, j, first):
                    prev = Pos(pos.const - per, pos.step, pos.i)
                    for s in range(per):
                        S_(pos, j, s, first)
                        if s >= 1:
                            T_(pos, s - 1)
                        elif not first:
                            T_(prev, per - 1)
                        if s >= 2:
                            V_(pos, j, s - 2)
                        elif not first:
                            V_(prev, j - 1, per - 2 + s)
                        if s == 3 and not first:
                            O_(prev, j - 1, at["split"] + j - 1)

                unit(Pos(t0), 0, True)
                if looped:
                    with pe.Fori(1, n) as j:
                        unit(Pos(t0, per, j), j, False)
                else:
                    for j in range(1, n):
                        unit(Pos(t0 + per * j), j, False)
                end = Pos(t0 + per * (n - 1))
                T_(end, per - 1)
                V_(end, n - 1, per - 2)
                V_(end, n - 1, per - 1)
                O_(end, n - 1, at["split"] + n - 1)
                pe.wait_ge(lo_done, at["split"] + n)

            def head_scores(keys):
                def scores(j, s):
                    hh, qb = s // 4, s % 4
                    w = (qb + 1) * P
                    k = keys[:, j, 0:w] if isinstance(j, int) else keys[:, bass.ds(j, 1), 0:w].rearrange("p a s -> p (a s)")
                    pe.matmul(ms[:, s % 2, 0:w], qs[:, hh, qb * P:qb * P + P], k, start=True, stop=False)
                    return pe.matmul(ms[:, s % 2, qb * P:w], identb[:], tri[:], start=False, stop=True)
                return scores

            def head_v(t):
                def v_of(j, s, kb):
                    if isinstance(j, int):
                        return t[:, kb, j * P + 64 * (s // 4):j * P + 64 * (s // 4) + 64]
                    return t[:, kb, bass.ds(j * P + 64 * (s // 4), 64)]
                return v_of

            def wait_copies(base):
                def before(j, s):
                    if s in (0, 4):
                        pe.wait_ge(q_copied, base + 2 * j + s // 4 + 1)
                return before

            attention(fox, 8, biased, [1, 2, 3, 4] * 2, head_scores(kT), head_v(v_s), 64, wait_copies(0), True)
            gemm(wo, A, ready=fox["split"])
            ffn_layer(1, B, A)

            def c_stats():
                stat(gqx, fin["acc"] + 7)
                col_stats()
            stat(None, gate[1]["acc"] + 7)
            gemm(gqx, A, n_slabs=2, ready=fin["split"], hook=c_stats)
            for c in range(4):
                wait_evac(pe, Pos(gqx["blk"]), c)

            def x_scores(j, s):
                return pe.matmul(ms[:, s % 2, 0:MEM], qx[:, j, s * P:s * P + P], mk[:, j, :], start=True, stop=True)
            attention(xat, 4, exped, [2] * 4, x_scores, lambda j, s, kb: mv[:, kb, j * P:j * P + P], P, None, False)

            def branch(n, k0, ysplit, kn):
                at = br[n]
                for half in range(2):
                    sl, bl = at["slab"] + 3 * half, at["blk"] + 8 * half
                    for s in range(2):
                        slab_ws(Pos(sl + s), Pos(bl + 2 * s), A)
                    pe.wait_ge(lo_done, ysplit + kn)
                    slab_ws(Pos(sl + 2), Pos(bl + 4), B, k0=k0, kk=4)

            branch(2, 4, xat["split"], 4)
            gemm(gxg, A)
            pe.wait_ge(wg_ready, 64)
            for j, (at, s) in enumerate(((gqm, 0), (gqm, 1), (gkm, 0), (gkm, 1))):
                pe.wait_ge(xa_c, 4 * (j + 1))
                if j:
                    pe.wait_ge(l_act, 4 * j - 2)
                pe.matmul(ms[:, 0, :], wga[:, j], xc[:, j], start=True, stop=True).then_inc(l_gate, 1)
                pe.matmul(ms[:, 1, :], wgx[:, j], xc[:, j], start=True, stop=True).then_inc(l_gate, 1)
                slab_ws(Pos(at["slab"] + s), Pos(at["blk"] + 2 * s), A)
            for s in range(2):
                slab_xs(Pos(gvm["slab"] + s), Pos(gvm["blk"] + 4 * s), A, 4)
            branch(0, 0, lru["split"], 4)
            for c in range(4):
                wait_evac(pe, Pos(br[0]["blk"] + 12), c)
            attention(mob, 4, biased, [1, 2, 3, 4] * 2, head_scores(km), head_v(vm), 64, wait_copies(16), True)
            branch(1, 4, mob["split"], 4)
            gemm(wout, A, ready=mrg["split"])
            f = ffn2
            src = wout
            gemm(f, B, n_slabs=2, ready=src["split"], hook=lambda: stat(f, src["acc"] + 7))
            with pe.Fori(0, 3) as i:
                for s in range(2):
                    slab_ws(Pos(f["slab"] + 2 + s, 2, i), Pos(f["blk"] + 4 + 2 * s, 4, i), B)
            with pe.Fori(0, 2) as i:
                for s in range(12):
                    slab_ws(Pos(f["slab"] + 8 + s, 12, i), Pos(f["blk"] + 16 + 2 * s, 24, i),
                            A if s < 4 else B, ready=Pos(f["split"], 8, i) if s == 0 else None)
            for s in range(4):
                slab_ws(Pos(f["slab"] + 32 + s), Pos(f["blk"] + 64 + 2 * s), A, ready=Pos(f["split"] + 16) if s == 0 else None)
            stat(None, f["acc"] + 7)

        @block.scalar
        def _(act):
            def next_w(sp_, bp):
                if not sp_.step and sp_.const + 1 >= NS:
                    return
                s = sp_.slot(2, 1)
                act.wait_ge(raw_ready[s], 16 * (sp_.turns(2, 1) + 1))
                if bp.const > 0:
                    act.wait_ge(blk_done, bp.at())
                act.activation(w_hi[:, s], raw[:, s], ACT.Copy).then_inc(w_hi_done, 1)

            def next_of(at, s, bs=None):
                next_w(Pos(at["slab"] + s), Pos(at["blk"] + (2 * s if bs is None else bs)))

            def square(c, at):
                if c >= 3:
                    act.wait_ge(acc_done, at["acc"] + c - 2)
                dst = acc_sq[:] if c == 0 else sqb[:, c % 2]
                act.activation(dst, h[:, c], ACT.Square).then_inc(sq_done, 1)

            def prep(c, X, gain, at, ready):
                ready()
                square(c, at)
                act.activation(X[0][:, c], h[:, c], ACT.Copy, scale=col(gain, c)).then_inc(hi_done, 1)

            def finish_norm(at):
                act.wait_ge(var_done, at["norm"] + 1)
                act.activation(rstd[:], var[:], ACT.Sqrt).then_inc(rstd_done, 1)

            def finish_col(n):
                act.wait_ge(col_var, n + 1)
                act.activation(rcol[:], colv[:], ACT.Sqrt).then_inc(col_done, 1)

            act.wait_ge(par_ready, 16)
            for c in range(8):
                prep(c, A, "mix0", x0, lambda: act.wait_ge(x_ready[c // 2], 16))
                if c == 1:
                    act.wait_ge(raw_ready[0], 16)
                    act.activation(w_hi[:, 0], raw[:, 0], ACT.Copy).then_inc(w_hi_done, 1)
            next_w(Pos(0), Pos(0))
            finish_norm(x0)
            act.wait_ge(mem_ready, 16)
            act.activation(mem_sq, mem_raw[:], ACT.Square).then_inc(msq_done, 1)

            def pw1_gates(bp, pcol):
                for s in range(2):
                    wait_evac(act, bp, 2 * s + 1)
                    act.activation(T[:, 2 * s + 1], T[:, 2 * s + 1], ACT.Sigmoid, bias=pcol("b_g1", s, 0)).then_inc(sg_done, 1)

            def tap_products(i, pcol):
                for t in range(POOL_TAPS):
                    for s in range(2):
                        src = upad[:, s, t:t + S]
                        if t == 0:
                            act.wait_ge(u_done, 2 * i + s + 1)
                            m = act.activation(pool_sum[:, s], src, ACT.Identity, scale=pcol("w_dw", s, 0), bias=pcol("b_dw", s, 0))
                        else:
                            if t >= 2:
                                act.wait_ge(pool_conv, 2 * (POOL_TAPS - 1) * i + 2 * t + s - 3)
                            m = act.activation(sqb[:, s], src, ACT.Copy, scale=pcol("w_dw", s, 8 * t))
                        m.then_inc(tap_done, 1)

            def col0(n, s, o):
                return col(n, o + s)
            next_w(Pos(1), Pos(2))
            pw1_gates(Pos(0), col0)
            next_w(Pos(2), Pos(4))
            tap_products(0, col0)
            next_w(Pos(3), Pos(6))
            act.wait_ge(mvar_done, 1)
            act.activation(U[:, 0, 0:MEM], var[:, 0:MEM], ACT.Sqrt).then_inc(mrstd_done, 1)
            act.wait_ge(mscaled, 8)
            act.activation(b_hi[:, :, 0:MEM], mem_raw[:], ACT.Copy).then_inc(mp_hi, 1)
            act.wait_ge(p_ready, 16)
            act.activation(p_hi0[:], p_raw0[:], ACT.Copy).then_inc(mp_hi, 1)
            with act.Fori(1, 4) as i:
                def coli(n, s, o):
                    return par[:, bass.ds(COL[n] + o + s + 2 * i, 1)]
                pw1_gates(Pos(0, 4, i), coli)
                next_w(Pos(2, 2, i), Pos(4, 4, i))
                tap_products(i, coli)
                next_w(Pos(3, 2, i), Pos(6, 4, i))
            for c in range(4):
                bp = Pos(memkv["blk"])
                wait_blk(act, bp, c)
                act.activation(mk[:, c, :], gp[:, bp.slot(4, c), 0:MEM], ACT.Copy).then_inc(evac[bp.slot(4, c)], 1)

            def memory_values(s):
                for t in range(2):
                    bp = Pos(memkv["blk"] + 4 + 2 * s)
                    wait_blk(act, bp, t)
                    act.activation(mv[:, t, 256 * s:256 * s + 256], gp[:, bp.slot(4, t), 0:256], ACT.Copy).then_inc(evac[bp.slot(4, t)], 1)
            next_of(memkv, 2)
            for k in range(8):
                act.wait_ge(centred, k + 1)
                if k >= 2:
                    act.wait_ge(cvar_done, k - 1)
                act.activation(sqb[:, k % 2], big[:, k], ACT.Square).then_inc(csq_done, 1)
            memory_values(0)
            next_of(memkv, 3)
            finish_norm(ln)
            memory_values(1)
            for k in range(8):
                act.wait_ge(normed, k + 1)
                if k >= 2:
                    act.wait_ge(lo_done, ln["split"] + k - 1)
                act.activation(U[:, k % 2], big[:, k], ACT.Silu, bias=col("ln_b", k), scale=col("ln_g", k)).then_inc(silu_done, 1)
                act.wait_ge(silu_done, k + 1)
                act.activation(b_hi[:, k], U[:, k % 2], ACT.Copy).then_inc(hi_done, 1)

            def add_and_prep(at, X, gain, split_at=None, bp0=None):
                for s in range(4):
                    next_of(at, s)
                    for c in range(2):
                        k = 2 * s + c
                        prep(k, X, gain, at, lambda: wait_evac(act, Pos(at["blk"]), k))
            add_and_prep(pw2, A, "ffn0")

            def up_hi(f, sp_, bp, fu, H_, k):
                next_w(sp_, bp)
                for c in range(2):
                    act.wait_ge(full, fu.at(k + c + 1))
                    act.activation(H_[0][:, k + c], U[:, (k + c) % 2], ACT.Copy).then_inc(hi_done, 1)

            def ffn_layer(l, X, H_):
                f = ffn[l]
                fu = f["full"]
                for s in range(4):
                    sp_, bp = Pos(f["slab"] + s), Pos(f["blk"] + 2 * s)
                    if s == 0:
                        next_w(sp_, bp)
                        finish_norm(pw2 if l == 0 else wo)
                        for c in range(2):
                            act.wait_ge(full, fu + c + 1)
                            act.activation(H_[0][:, c], U[:, c % 2], ACT.Copy).then_inc(hi_done, 1)
                    else:
                        up_hi(f, sp_, bp, Pos(fu), H_, 2 * s)
                with act.Fori(0, 3) as i:
                    for s in range(4):
                        next_w(Pos(f["slab"] + 4 + s, 8, i), Pos(f["blk"] + 8 + 2 * s, 16, i))
                    for s in range(4):
                        up_hi(f, Pos(f["slab"] + 8 + s, 8, i), Pos(f["blk"] + 16 + 2 * s, 16, i), Pos(fu + 8, 8, i), H_, 2 * s)
                for s in range(4):
                    next_of(f, 28 + s)
                    for c in range(2):
                        k = 2 * s + c
                        prep(k, X, "ple%d" % l, f, lambda: wait_evac(act, Pos(f["blk"] + 56), k))
                next_of(proj[l], 0)
                for c in range(8):
                    bp = Pos(proj[l]["blk"])
                    wait_blk(act, bp, c)
                    act.activation(bigs[l][:, c], gp[:, bp.slot(4, c)], ACT.Copy).then_inc(evac[bp.slot(4, c)], 1)
                g = gate[l]
                for c in range(9):
                    if c < 8:
                        if c % 2 == 0:
                            next_of(g, c // 2)
                        if c == 0:
                            finish_norm(f)
                        wait_evac(act, Pos(g["blk"]), c)
                        act.activation(T[:, c % 2], T[:, c % 2], ACT.Sigmoid).then_inc(sg_done, 1)
                    if c >= 1:
                        act.wait_ge(hg_done, g["hg"] + c)
                        if l == 0:
                            prep(c - 1, B, "mix1", g, lambda: None)
                        else:
                            square(c - 1, g)
            ffn_layer(0, A, B)

            act.wait_ge(blk_done, gate[0]["blk"] + 8)
            for s in range(4):
                next_of(gq, s)
                if s == 0:
                    finish_norm(gate[0])
                    finish_col(0)
                for k in range(3 * s, min(3 * s + 3, 8)):
                    act.activation(a_hi[:, k], h[:, k], ACT.Copy, scale=col("kv", k)).then_inc(hi_done, 1)
                if s == 2:
                    act.wait_ge(wf_ready, 16)
                    act.wait_ge(wf_zero, 2)
                    act.activation(wf_hi[:, :, 0:16], wf[:], ACT.Copy).then_inc(wf_hi_done, 1)
            for s in range(4):
                next_of(gk, s)
                if s == 0:
                    act.wait_ge(f_v, 2)
                    act.activation(T[0:16, 2], T[0:16, 1], ACT.Exp, scale=-1.0).then_inc(f_exp, 1)
            for s in range(4):
                next_of(gv, s, 4 * s)

            def attention(at, X, k0, n, per, looped, exp, pt_w, boundary=None):
                t0 = at["step"]

                def E_(pos, s, fresh):
                    act.wait_ge(biased, pos.at(s + 1))
                    if not fresh:
                        act.wait_ge(o_done, pos.at(s - 3))
                    exp(s).then_inc(exped, 1)

                def C_(pos, s, fresh):
                    w = pt_w[s % per]
                    act.wait_ge(transposed, pos.at(s + 1))
                    if not fresh:
                        act.wait_ge(pv_done, pos.at(s - 1))
                    act.activation(probT[:, s % 2, 0:w], ms[:, 2 + s % 2, 0:w], ACT.Copy).then_inc(pt_copied, 1)

                def H_(j):
                    act.wait_ge(ot_done, at["unit"] + j + 1)
                    dst = X[0][:, k0 + j] if isinstance(j, int) else X[0][:, bass.ds(k0 + j, 1)].rearrange("p a s -> p (a s)")
                    act.activation(dst, gp[:, 2], ACT.Copy).then_inc(hi_done, 1)

                def unit(pos, j, first):
                    prev = Pos(pos.const - per, pos.step, pos.i)
                    for s in range(per):
                        if boundary:
                            boundary(j, s, first)
                        E_(pos, s, first and s < 4)
                        if s >= 1:
                            C_(pos, s - 1, first and s - 1 < 2)
                        elif not first:
                            C_(prev, per - 1, False)
                        if s == 3 and not first:
                            H_(j - 1)
                unit(Pos(t0), 0, True)
                if looped:
                    with act.Fori(1, n) as j:
                        unit(Pos(t0, per, j), j, False)
                else:
                    for j in range(1, n):
                        unit(Pos(t0 + per * j), j, False)
                C_(Pos(t0 + per * (n - 1)), per - 1, False)
                H_(n - 1)

            def head_exp(s):
                w = (s % 4 + 1) * P
                return act.activation(prob[:, s % 2, 0:w], prob[:, s % 2, 0:w], ACT.Exp, scale=-1.0,
                                      bias=nmax[:, s % 2:s % 2 + 1], accum_out=rsum[:, s % 4:s % 4 + 1])
            causal = [P, 2 * P, 3 * P, 4 * P] * 2
            attention(fox, A, 0, 8, 8, True, head_exp, causal)
            add_and_prep(wo, B, "ffn1")
            act.wait_ge(p_ready, 32)
            act.activation(p_hi1[:], p_raw1[:], ACT.Copy).then_inc(hi_done, 1)
            ffn_layer(1, B, A)

            finish_norm(gate[1])
            for k in range(8):
                prep(k, A, "mix2", fin, lambda: act.wait_ge(fin_done, k + 1))
            for s in range(2):
                next_of(gqx, s)
                if s == 0:
                    finish_norm(fin)
                    finish_col(1)
            act.wait_ge(sp_chain, 1)
            act.activation(sp[:, 1], sp[:, 0], ACT.Exp, scale=-1.0).then_inc(sp_e, 1)

            def x_exp(s):
                return act.activation(prob[:, s % 2, 0:MEM], ms[:, s % 2, 0:MEM], ACT.Exp,
                                      bias=nmax[:, s % 2:s % 2 + 1], accum_out=rsum[:, s % 4:s % 4 + 1])
            attention(xat, B, 4, 4, 4, False, x_exp, [MEM] * 4)

            def branch(n):
                at = br[n]
                for half in range(2):
                    bp = Pos(at["blk"] + 8 * half)
                    for s in range(3):
                        next_w(Pos(at["slab"] + 3 * half + s), Pos(at["blk"] + 8 * half + 2 * s))
                        if s < 2:
                            for c in range(2 * s, 2 * s + 2):
                                wait_evac(act, bp, c)
                                act.activation(T[:, c], T[:, c], ACT.Sigmoid).then_inc(sg_done, 1)
            branch(2)
            for s in range(4):
                next_of(gxg, s)
            for j in range(4):
                wait_evac(act, Pos(gxg["blk"] + 4), j)
                act.activation(ga[:, j], ga[:, j], ACT.Gelu_apprx_tanh).then_inc(gelu_done, 1)
            def lru_hi(j):
                act.wait_ge(l_y, j + 1)
                act.activation(b_hi[:, j], U[:, 0], ACT.Copy).then_inc(hi_done, 1)

            for j, (at, s) in enumerate(((gqm, 0), (gqm, 1), (gkm, 0), (gkm, 1))):
                next_of(at, s)
                if j:
                    act.wait_ge(l_chain, 7 * j)
                    lru_hi(j - 1)
                for r, b in ((0, "lru_ba"), (1, "lru_bx")):
                    act.wait_ge(l_gate, 2 * j + r + 1)
                    act.activation(T[:, r], ms[:, r], ACT.Sigmoid, bias=col(b, j)).then_inc(l_act, 1)
                act.wait_ge(l_act, 4 * j + 1)
                if j == 0:
                    act.wait_ge(sp_chain, 20)
                act.activation(T[:, 2], T[:, 0], ACT.Tanh, scale=sp[:, 7, j:j + 1]).then_inc(l_act, 1)
                act.wait_ge(l_act, 4 * j + 3)
                act.activation(T[:, 3], T[:, 2], ACT.Sqrt).then_inc(l_act, 1)
            for s in range(2):
                next_of(gvm, s, 4 * s)
                if s == 0:
                    lru_hi(3)
            branch(0)

            def mob_bias(j, hh, first):
                if not first:
                    act.wait_ge(biased, mob["step"] + 8 * j - 8 + 4 * (hh + 1))
                sl = col("slope", 2 * j + hh) if isinstance(j, int) else par[:, bass.ds(COL["slope"] + 2 * j + hh, 1)]
                act.activation(mbias[:, hh], dist[:], ACT.Copy, scale=sl).then_inc(mb_ready, 1)

            def mob_boundary(j, s, first):
                if s == 0 and not first:
                    mob_bias(j, 0, False)
                    mob_bias(j, 1, False)
            act.wait_ge(dist_ready, 2)
            mob_bias(0, 0, True)
            mob_bias(0, 1, True)
            attention(mob, B, 4, 4, 8, True, head_exp, causal, mob_boundary)
            branch(1)
            for k in range(8):
                act.wait_ge(gm_done, br[1]["gm"] + 8 if k == 0 else br[1]["gm"] + 8)
                act.activation(a_hi[:, k], merged[:, k], ACT.Copy).then_inc(hi_done, 1)
            add_and_prep(wout, B, "ffn2")

            f = ffn2

            def gu(sp_, bp, gl, fu, k):
                next_w(sp_, bp)
                if bp.const == f["blk"]:
                    finish_norm(wout)
                act.wait_ge(g_chain, gl.at(3 * (k + 1)))
                cb = gl
                i = gl.i
                bias = col("cb", k) if not gl.step else par[:, bass.ds(COL["cb"] + 8 + k + 8 * i, 1)]
                act.activation(T[:, k % 2], T[:, k % 2], ACT.Gelu_apprx_tanh, bias=bias).then_inc(gelu_done, 1)
                act.wait_ge(full, fu.at(k + 1))
                act.activation(a_hi[:, k], U[:, k % 2], ACT.Copy).then_inc(hi_done, 1)
            for k in range(8):
                gu(Pos(f["slab"] + k), Pos(f["blk"] + 2 * k), Pos(0), Pos(f["full"]), k)
            with act.Fori(0, 2) as i:
                for s in range(4):
                    next_w(Pos(f["slab"] + 8 + s, 12, i), Pos(f["blk"] + 16 + 2 * s, 24, i))
                for k in range(8):
                    gu(Pos(f["slab"] + 12 + k, 12, i), Pos(f["blk"] + 24 + 2 * k, 24, i), Pos(24, 24, i), Pos(f["full"] + 8, 8, i), k)
            for s in range(4):
                next_of(f, 32 + s)
                for c in range(2):
                    k = 2 * s + c
                    wait_evac(act, Pos(f["blk"] + 64), k)
                    square(k, f)
            finish_norm(f)

        @block.vector
        def _(v):
            def tt(o, a, b, op):
                return v.tensor_tensor(o, a, b, op)

            def stt(o, a, s, b, op0, op1):
                return v.scalar_tensor_tensor(o, a, s, b, op0, op1)

            def low(at, n, o, full_ap, hi):
                v.wait_ge(hi_done, at + n + 1)
                tt(o, full_ap, f32(hi), ALU.subtract).then_inc(lo_done, 1)

            def low_h(at, k, X, gain):
                v.wait_ge(hi_done, at["split"] + (k if at is not None else 0) + 1)
                stt(X[1][:, k], h[:, k], col(gain, k), f32(X[0][:, k]), ALU.mult, ALU.subtract).then_inc(lo_done, 1)

            def add_square(at, k):
                if k == 0:
                    return
                v.wait_ge(sq_done, at["sq"] + k + 1)
                if k >= 2:
                    v.wait_ge(acc_done, at["acc"] + k - 1)
                tt(acc_sq[:], acc_sq[:], sqb[:, k % 2], ALU.add).then_inc(acc_done, 1)

            def prep(at, k, X, gain, soff=0):
                v.wait_ge(hi_done, at["split"] + soff + k + 1)
                stt(X[1][:, k], h[:, k], col(gain, k), f32(X[0][:, k]), ALU.mult, ALU.subtract).then_inc(lo_done, 1)
                add_square(at, k)

            def finish_var(at):
                v.wait_ge(eps_done, at["norm"] + 1)
                v.reciprocal(var[:], var[:]).then_inc(var_done, 1)

            def norm(at):
                v.wait_ge(stat_done, at["stat"] + 1)
                if at["norm"]:
                    v.wait_ge(rstd_done, at["norm"])
                v.tensor_scalar(var[:], ms[:, 0], EPS, None, ALU.add).then_inc(eps_done, 1)
                finish_var(at)

            def norm_col(n):
                v.wait_ge(col_stat, n + 1)
                v.tensor_scalar(colv[:], ms[:, 1, 0:QB], EPS, None, ALU.add).then_inc(col_eps, 1)
                v.wait_ge(col_eps, n + 1)
                v.reciprocal(colv[:], colv[:]).then_inc(col_var, 1)

            def scaled(o, bp, c, rows=P):
                wait_blk(v, bp, c)
                b = bp.slot(4, c)
                tt(o, gp[:, b], rstd[:], ALU.mult).then_inc(evac[b], 1)

            v.wait_ge(par_ready, 16)
            for k in range(8):
                prep(x0, k, A, "mix0")
            norm(x0)
            v.wait_ge(rstd_done, 1)

            v.wait_ge(pad_zero, 1)

            def pw1_pair(bp, u0, cv, pc, pcol, dst, mem_norm=False):
                for s in range(2):
                    scaled(T[:, 2 * s], bp, 2 * s)
                    scaled(T[:, 2 * s + 1], bp, 2 * s + 1)
                for s in range(2):
                    v.wait_ge(sg_done, u0.at(s + 1))
                    wait_evac(v, bp, 2 * s)
                    if cv.step:
                        v.wait_ge(conv_done, cv.at())
                        v.wait_ge(tap_done, 2 * POOL_TAPS * (cv.i + 1))
                    stt(upad[:, s, TAPS - 1:], T[:, 2 * s], pcol("b_a1", s, 0), T[:, 2 * s + 1], ALU.add, ALU.mult).then_inc(u_done, 1)
                for n in range(TAPS - POOL_TAPS):
                    for s in range(2):
                        t = POOL_TAPS + n
                        src, sum_ = upad[:, s, t:t + S], ms[:, 3 * s]
                        if n == 0:
                            v.wait_ge(u_done, u0.at(s + 1))
                            m = v.tensor_scalar(sum_, src, pcol("w_dw", s, 8 * t), None, ALU.mult)
                        else:
                            v.wait_ge(conv_done, cv.at(2 * n + s - 1))
                            m = stt(sum_, src, pcol("w_dw", s, 8 * t), sum_, ALU.mult, ALU.add)
                        m.then_inc(conv_done, 1)
                        if mem_norm and n == 2 and s == 0:
                            v.wait_ge(mstat_done, 1)
                            v.tensor_scalar(var[:, 0:MEM], ms[:, 1, 0:MEM], EPS, None, ALU.add).then_inc(meps_done, 1)
                        if mem_norm and n == 4 and s == 0:
                            v.wait_ge(meps_done, 1)
                            v.reciprocal(var[:, 0:MEM], var[:, 0:MEM]).then_inc(mvar_done, 1)
                for s in range(2):
                    v.wait_ge(conv_done, cv.at(CONV_OPS - 3 + s))
                    v.wait_ge(pool_conv, pc.at(2 * POOL_TAPS - 3 + s))
                    tt(dst(s), ms[:, 3 * s], pool_sum[:, s], ALU.add).then_inc(conv_done, 1)
            pw1_pair(Pos(0), Pos(0), Pos(0), Pos(0), lambda n, s, o: col(n, o + s), lambda s: big[:, s],
                     mem_norm=True)
            v.wait_ge(mrstd_done, 1)
            for k in range(8):
                stt(mem_raw[:, k], mem_raw[:, k], col("memg", k), U[:, 0, 0:MEM], ALU.mult, ALU.mult).then_inc(mscaled, 1)
            with v.Fori(0, 3) as i:
                pw1_pair(Pos(4, 4, i), Pos(2, 2, i), Pos(CONV_OPS, CONV_OPS, i), Pos(2 * POOL_TAPS - 2, 2 * POOL_TAPS - 2, i),
                         lambda n, s, o: par[:, bass.ds(COL[n] + o + 2 + s + 2 * i, 1)],
                         lambda s: big[:, bass.ds(2 + s + 2 * i, 1)].rearrange("p a s -> p (a s)"))
            v.wait_ge(mean_done, 1)
            for k in range(8):
                tt(big[:, k], big[:, k], ms[:, 1], ALU.subtract).then_inc(centred, 1)
            v.wait_ge(cvar_done, 8)
            v.tensor_scalar(var[:], ms[:, 2], EPS, None, ALU.add).then_inc(eps_done, 1)
            finish_var(ln)
            v.wait_ge(rstd_done, ln["norm"] + 1)
            for k in range(9):
                if k < 8:
                    tt(big[:, k], big[:, k], rstd[:], ALU.mult).then_inc(normed, 1)
                if k >= 1:
                    low(ln["split"], k - 1, b_lo[:, k - 1], U[:, (k - 1) % 2], b_hi[:, k - 1])
            for k in range(9):
                if k < 8:
                    bp = Pos(pw2["blk"])
                    wait_blk(v, bp, k)
                    stt(h[:, k], gp[:, bp.slot(4, k)], col("b_pw2", k), h[:, k], ALU.add, ALU.add).then_inc(evac[bp.slot(4, k)], 1)
                if k >= 1:
                    prep(pw2, k - 1, A, "ffn0")

            def up_block(bp, c, fu, spl, H_, k):
                scaled(T[:, k % 4], bp, c)
                wait_evac(v, bp, c)
                stt(U[:, k % 2], T[:, k % 4], 0.0, T[:, k % 4], ALU.max, ALU.mult).then_inc(full, 1)
                if k >= 1:
                    low_hid(spl, H_, k - 1)

            def low_hid(spl, H_, k):
                v.wait_ge(hi_done, spl.at(k + 1))
                tt(H_[1][:, k], U[:, k % 2], f32(H_[0][:, k]), ALU.subtract).then_inc(lo_done, 1)

            def add_h(bp, k):
                wait_blk(v, bp, k)
                b = bp.slot(4, k)
                tt(h[:, k], gp[:, b], h[:, k], ALU.add).then_inc(evac[b], 1)

            def ffn_layer(l, X, H_):
                f = ffn[l]
                n = pw2 if l == 0 else wo
                norm(n)
                v.wait_ge(rstd_done, n["norm"] + 1)
                for k in range(8):
                    up_block(Pos(f["blk"]), k, None, Pos(f["split"]), H_, k)
                low_hid(Pos(f["split"]), H_, 7)
                with v.Fori(0, 3) as i:
                    for k in range(8):
                        add_h(Pos(f["blk"] + 8, 16, i), k)
                    for k in range(8):
                        up_block(Pos(f["blk"] + 16, 16, i), k, None, Pos(f["split"] + 8, 8, i), H_, k)
                    low_hid(Pos(f["split"] + 8, 8, i), H_, 7)
                for k in range(9):
                    if k < 8:
                        add_h(Pos(f["blk"] + 56), k)
                    if k >= 1:
                        prep(f, k - 1, X, "ple%d" % l, soff=32)
                g = gate[l]
                norm(f)
                v.wait_ge(rstd_done, f["norm"] + 1)
                bp = Pos(g["blk"])
                scaled(T[:, 0], bp, 0)
                for c in range(9):
                    if c < 7:
                        scaled(T[:, (c + 1) % 2], bp, c + 1)
                    if c < 8:
                        v.wait_ge(sg_done, g["sg"] + c + 1)
                        tt(T[:, 2 + c % 2], T[:, c % 2], bigs[l][:, c], ALU.mult).then_inc(gm_done, 1)
                        v.wait_ge(gm_done, g["gm"] + c + 1)
                        tt(h[:, c], h[:, c], T[:, 2 + c % 2], ALU.add).then_inc(hg_done, 1)
                    if c >= 1:
                        if l == 0:
                            prep(g, c - 1, B, "mix1")
                        else:
                            add_square(g, c - 1)
            ffn_layer(0, A, B)

            norm(gate[0])
            norm_col(0)
            v.wait_ge(rstd_done, gate[0]["norm"] + 1)
            for k in range(8):
                bp = Pos(gq["blk"])
                wait_blk(v, bp, k)
                b = bp.slot(4, k)
                stt(qT[:, k], gp[:, b], 0.125, rstd[:], ALU.mult, ALU.mult).then_inc(evac[b], 1)
                for n in range(2 * k - 2, min(2 * k, 8)):
                    if n >= 0:
                        low_h(kvsplit, n, A, "kv")
                if k == 5:
                    v.wait_ge(wf_hi_done, 1)
                    tt(wf_lo[:, :, 0:16], wf[:], f32(wf_hi[:, :, 0:16]), ALU.subtract).then_inc(wf_split, 1)

            def v_blocks(at, dst, n):
                for s in range(n):
                    for t in range(QB):
                        bp = Pos(at["blk"] + 4 * s)
                        wait_blk(v, bp, t)
                        b = bp.slot(4, t)
                        v.tensor_scalar(dst[:, t, 256 * s:256 * s + 256], gp[:, b, 0:256], rcol[:, t:t + 1], None,
                                        ALU.mult).then_inc(evac[b], 1)
            R = slice(0, 16)
            f_, ax, e, z, z2, pl = T[R, 0], T[R, 1], T[R, 2], T[R, 3], U[R, 0], U[R, 1]
            chain = [0]

            def link(ins):
                chain[0] += 1
                ins.then_inc(f_chain, 1)
                v.wait_ge(f_chain, chain[0])

            def log1p_z(e, z, z2, rd, lk):
                lk(v.tensor_scalar(z2, e, 2.0, None, ALU.add))
                lk(v.reciprocal(rd, z2))
                lk(tt(z, e, rd, ALU.mult))
                lk(tt(z2, z, z, ALU.mult))

            def log1p_series(z, z2, pl, lk):
                lk(v.tensor_scalar(pl, z2, ATANH[-1], None, ALU.mult))
                for cf in ATANH[-2::-1]:
                    lk(stt(pl, pl, cf, z2, ALU.add, ALU.mult))
                lk(stt(pl, pl, 1.0, z, ALU.add, ALU.mult))

            for k in range(8):
                scaled(kT[:, k], Pos(gk["blk"]), k)
                if k == 0:
                    v.wait_ge(f_stat, 1)
                    link(tt(f_, ms[R, 2], rstd[R], ALU.mult))
                    v.tensor_scalar(f_, f_, par[R, COL["b_f"]:COL["b_f"] + 1], None, ALU.add).then_inc(f_v, 1)
                    v.wait_ge(f_v, 1)
                    stt(ax, f_, -1.0, f_, ALU.mult, ALU.max).then_inc(f_v, 1)
                if k == 1:
                    v.wait_ge(f_exp, 1)
                    log1p_z(e, z, z2, ax, link)
                if k == 3:
                    log1p_series(z, z2, pl, link)
                if k == 5:
                    link(v.tensor_scalar(f_, f_, 0.0, None, ALU.min))
                    link(stt(pl, pl, 2.0, f_, ALU.mult, ALU.subtract))
                    link(v.memset(z2, 1.0))
                    v.tensor_tensor_scan(z, z2, pl, 0.0, ALU.mult, ALU.add).then_inc(f_v, 1)
            v.wait_ge(col_done, 1)
            v_blocks(gv, v_s, 4)

            def attention(at, X, k0, n, per, looped, bias, ow, qb_of, col_of):
                t0 = at["step"]

                def B_(pos, j, s, fresh):
                    v.wait_ge(scored, pos.at(s + 1))
                    if not fresh:
                        v.wait_ge(transposed, pos.at(s - 1))
                    bias(j, s).then_inc(biased, 1)

                def N_(pos, j, s):
                    if s == 0 and not (isinstance(j, int) and j == 0):
                        v.wait_ge(ot_done, at["unit"] + j)
                    v.wait_ge(exped, pos.at(s + 1))
                    v.reciprocal(rinv[:, s % 4:s % 4 + 1], rsum[:, s % 4:s % 4 + 1]).then_inc(sum_inv, 1)
                    v.wait_ge(sum_inv, pos.at(s + 1))
                    v.wait_ge(pv_done, pos.at(s + 1))
                    c0 = col_of(s)
                    v.tensor_scalar(o_sb[:, qb_of(s), c0:c0 + ow], gp[:, s % 2, 0:ow], rinv[:, s % 4:s % 4 + 1], None,
                                    ALU.mult).then_inc(o_done, 1)

                def L_(j):
                    v.wait_ge(hi_done, at["split"] + j + 1)
                    at_ = (lambda t: t[:, k0 + j]) if isinstance(j, int) else (
                        lambda t: t[:, bass.ds(k0 + j, 1)].rearrange("p a s -> p (a s)"))
                    tt(at_(X[1]), gp[:, 2], f32(at_(X[0])), ALU.subtract).then_inc(lo_done, 1)

                def unit(pos, j, first):
                    prev = Pos(pos.const - per, pos.step, pos.i)
                    for s in range(per):
                        B_(pos, j, s, first and s < 2)
                        if s >= 3:
                            N_(pos, j, s - 3)
                        elif not first:
                            N_(prev, j - 1, per - 3 + s)
                        if s == 3 and not first:
                            L_(j - 1)
                unit(Pos(t0), 0, True)
                if looped:
                    with v.Fori(1, n) as j:
                        unit(Pos(t0, per, j), j, False)
                else:
                    for j in range(1, n):
                        unit(Pos(t0 + per * j), j, False)
                for s in range(per - 3, per):
                    N_(Pos(t0 + per * (n - 1)), n - 1, s)
                L_(n - 1)

            def head_bias(b_of, ready):
                def bias(j, s):
                    hh, qb = s // 4, s % 4
                    if qb == 0:
                        ready(j, hh)
                    w = (qb + 1) * P
                    v.sem_inc(step_open, 1)
                    return v.tensor_tensor_reduce(prob[:, s % 2, 0:w], ms[:, s % 2, 0:w], b_of(hh, qb, w), -1.0, 3e38,
                                                  ALU.add, ALU.min, nmax[:, s % 2:s % 2 + 1])
                return bias
            attention(fox, A, 0, 8, 8, True,
                      head_bias(lambda hh, qb, w: fbias[:, hh, 0:w], lambda j, hh: v.wait_ge(bias_ready[hh], 16 * (j + 1))),
                      64, lambda s: s % 4, lambda s: 64 * (s // 4))
            for k in range(9):
                if k < 8:
                    add_h(Pos(wo["blk"]), k)
                if k >= 1:
                    prep(wo, k - 1, B, "ffn1")
            low(p_split[1]["split"], 0, p_lo1[:], p_raw1[:], p_hi1[:])
            ffn_layer(1, B, A)

            chain_sp = [0]

            def link_sp(ins):
                chain_sp[0] += 1
                ins.then_inc(sp_chain, 1)
                v.wait_ge(sp_chain, chain_sp[0])
            lam = par[:, COL["lam"]:COL["lam"] + 4]
            norm(gate[1])
            v.wait_ge(rstd_done, gate[1]["norm"] + 1)
            for k in range(9):
                if k < 8:
                    stt(h[:, k], h[:, k], col("final1", k), rstd[:], ALU.mult, ALU.mult).then_inc(fin_done, 1)
                if k >= 1:
                    prep(fin, k - 1, A, "mix2")
            norm(fin)
            norm_col(1)
            link_sp(stt(sp[:, 0], lam, -1.0, lam, ALU.mult, ALU.max))
            v.wait_ge(sp_e, 1)
            log1p_z(sp[:, 1], sp[:, 2], sp[:, 3], sp[:, 5], link_sp)
            log1p_series(sp[:, 2], sp[:, 3], sp[:, 4], link_sp)
            link_sp(v.tensor_scalar(sp[:, 6], lam, -1.0, 0.0, ALU.mult, ALU.max))
            link_sp(stt(sp[:, 6], sp[:, 4], 2.0, sp[:, 6], ALU.mult, ALU.add))
            link_sp(v.tensor_scalar(sp[:, 7], sp[:, 6], 4.0, None, ALU.mult))
            while chain_sp[0] < 20:
                link_sp(stt(sp[:, 0], lam, -1.0, lam, ALU.mult, ALU.max))
            assert chain_sp[0] == 20
            v.wait_ge(rstd_done, fin["norm"] + 1)
            for k in range(4):
                bp = Pos(gqx["blk"])
                wait_blk(v, bp, k)
                stt(qx[:, k], gp[:, bp.slot(4, k)], float(P) ** -0.5, rstd[:], ALU.mult, ALU.mult).then_inc(evac[bp.slot(4, k)], 1)

            def x_max(j, s):
                return v.tensor_reduce(nmax[:, s % 2:s % 2 + 1], ms[:, s % 2, 0:MEM], AX.X, ALU.max, negate=True)
            attention(xat, B, 4, 4, 4, False, x_max, P, lambda s: s, lambda s: 0)

            def branch(n, last=False):
                at = br[n]
                for half in range(2):
                    bp = Pos(at["blk"] + 8 * half)
                    if n != 2 and half:
                        v.wait_ge(gm_done, at["gm"] + 4)
                    for c in range(4):
                        scaled(T[:, c], bp, c)
                    for c in range(4):
                        v.wait_ge(sg_done, at["sg"] + 4 * half + c + 1)
                        wait_blk(v, bp, 4 + c)
                        b, m = bp.slot(4, 4 + c), merged[:, 4 * half + c]
                        if n == 2:
                            tt(m, gp[:, b], T[:, c], ALU.mult).then_inc(evac[b], 1)
                        else:
                            tt(T[:, c], gp[:, b], T[:, c], ALU.mult).then_inc(evac[b], 1)
                            wait_evac(v, bp, 4 + c)
                            tt(m, m, T[:, c], ALU.add).then_inc(gm_done, 1)
            branch(2)
            v.wait_ge(pad_zero, 2)
            for j in range(4):
                scaled(xap[:, j, 3:], Pos(gxg["blk"]), j)
            for j in range(4):
                scaled(ga[:, j], Pos(gxg["blk"] + 4), j)
                for t in range(4):
                    src = xap[:, j, t:t + S]
                    if t == 0:
                        wait_evac(v, Pos(gxg["blk"]), j)
                        m = v.tensor_scalar(xc[:, j], src, col("lru_w", j), col("lru_b", j), ALU.mult, ALU.add)
                    else:
                        v.wait_ge(xa_c, 4 * j + t)
                        m = stt(xc[:, j], src, col("lru_w", 4 * t + j), xc[:, j], ALU.mult, ALU.add)
                    m.then_inc(xa_c, 1)
            lch = [0]

            def link_l(ins):
                lch[0] += 1
                ins.then_inc(l_chain, 1)
                v.wait_ge(l_chain, lch[0])
            for j in range(4):
                v.wait_ge(l_act, 4 * j + 3)
                if j:
                    v.wait_ge(lo_done, lru["split"] + j)
                link_l(v.tensor_scalar(U[:, 0], T[:, 2], 1.0, None, ALU.add))
                link_l(v.reciprocal(U[:, 0], U[:, 0]))
                link_l(v.tensor_scalar(T[:, 0], U[:, 0], 2.0, -1.0, ALU.mult, ALU.add))
                v.wait_ge(l_act, 4 * j + 4)
                link_l(tt(T[:, 3], T[:, 3], U[:, 0], ALU.mult))
                link_l(stt(T[:, 3], T[:, 3], 2.0, T[:, 1], ALU.mult, ALU.mult))
                link_l(tt(T[:, 3], T[:, 3], xc[:, j], ALU.mult))
                link_l(v.tensor_tensor_scan(U[:, 1], T[:, 0], T[:, 3], 0.0, ALU.mult, ALU.add))
                v.wait_ge(gelu_done, j + 1)
                tt(U[:, 0], U[:, 1], ga[:, j], ALU.mult).then_inc(l_y, 1)
                if j == 0:
                    v.wait_ge(xa_c, 16)
                for k in range(2 * (j % 2), 2 * (j % 2) + 2):
                    if j < 2:
                        bp = Pos(gqm["blk"])
                        wait_blk(v, bp, k)
                        b = bp.slot(4, k)
                        stt(qm[:, k], gp[:, b], 0.125, rstd[:], ALU.mult, ALU.mult).then_inc(evac[b], 1)
                    else:
                        scaled(km[:, k], Pos(gkm["blk"]), k)
                low(lru["split"], j, b_lo[:, j], U[:, 0], b_hi[:, j])
            v.wait_ge(lo_done, lru["split"] + 4)
            v.wait_ge(col_done, 2)
            v_blocks(gvm, vm, 2)
            branch(0)
            attention(mob, B, 4, 4, 8, True,
                      head_bias(lambda hh, qb, w: mbias[:, hh, 3 * P - qb * P:3 * P - qb * P + w],
                                lambda j, hh: v.wait_ge(mb_ready, 2 * j + hh + 1)),
                      64, lambda s: s % 4, lambda s: 64 * (s // 4))
            branch(1)
            for k in range(8):
                low(mrg["split"], k, a_lo[:, k], merged[:, k], a_hi[:, k])
            for k in range(9):
                if k < 8:
                    add_h(Pos(wout["blk"]), k)
                if k >= 1:
                    prep(wout, k - 1, B, "ffn2")

            f = ffn2
            norm(wout)
            v.wait_ge(rstd_done, wout["norm"] + 1)
            v.wait_ge(pad_zero, 3)

            def gu(bp, gl, ge, spl, k, w_of):
                g = k % 2
                scaled(gpad[:, g, 2:], bp, 2 * k)
                wait_evac(v, bp, 2 * k)
                v.tensor_scalar(T[:, g], gpad[:, g, 0:S], w_of(k, 0), None, ALU.mult).then_inc(g_chain, 1)
                for t in range(1, 3):
                    v.wait_ge(g_chain, gl.at(3 * k + t))
                    stt(T[:, g], gpad[:, g, t:t + S], w_of(k, t), T[:, g], ALU.mult, ALU.add).then_inc(g_chain, 1)
                scaled(T[:, 2 + g], bp, 2 * k + 1)
                v.wait_ge(gelu_done, ge.at(k + 1))
                wait_evac(v, bp, 2 * k + 1)
                tt(U[:, g], T[:, 2 + g], T[:, g], ALU.mult).then_inc(full, 1)
                if k >= 1:
                    low_hid(spl, A, k - 1)
                if k == 7:
                    low_hid(spl, A, 7)
            for k in range(8):
                gu(Pos(f["blk"]), Pos(0), Pos(4), Pos(f["split"]), k, lambda k, t: col("cw", 24 * t + k))
            with v.Fori(0, 2) as i:
                for k in range(8):
                    add_h(Pos(f["blk"] + 16, 24, i), k)
                for k in range(8):
                    gu(Pos(f["blk"] + 24, 24, i), Pos(24, 24, i), Pos(12, 8, i), Pos(f["split"] + 8, 8, i), k,
                       lambda k, t: par[:, bass.ds(COL["cw"] + 24 * t + 8 + k + 8 * i, 1)])
            for k in range(9):
                if k < 8:
                    add_h(Pos(f["blk"] + 64), k)
                if k >= 1:
                    add_square(f, k - 1)
            norm(f)
            v.wait_ge(rstd_done, f["norm"] + 1)
            for k in range(8):
                stt(h[:, k], h[:, k], col("final2", k), rstd[:], ALU.mult, ALU.mult).then_inc(out_ready, 1)


def _tiles(w, rows, cols):
    import numpy as np
    w = np.concatenate([w[:, c:c + P] for c in cols], axis=1)
    return w.reshape(rows, P, len(cols) * P).transpose(1, 0, 2).reshape(P, SLAB)


def _slabs(i):
    import numpy as np
    out = []

    def plain(w, c0=0, c1=None, rows=8):
        per = 16 // rows
        c1 = w.shape[1] if c1 is None else c1
        for c in range(c0, c1, per * P):
            out.append(_tiles(w, rows, [c + P * n for n in range(per)]))

    def pairs(w0, w1, cols0, cols1):
        for a, b in zip(cols0, cols1):
            out.append(np.concatenate([w0[:, a:a + P], w1[:, b:b + P]], axis=1)
                       .reshape(8, P, 2 * P).transpose(1, 0, 2).reshape(P, SLAB))

    pw1 = i["conv_w_pw1"][0]
    pairs(pw1, pw1, range(0, D, P), range(D, 2 * D, P))
    plain(i["w_mem_kv_2"][0])
    plain(i["conv_w_pw2"][0])

    def ffn(l):
        for c in range(4):
            plain(i["ffn_w1"][l], c * D, (c + 1) * D)
            plain(i["ffn_w2"][l][c * D:(c + 1) * D])
        plain(i["ple_w_proj"][l], rows=2)
        plain(i["ple_w_gate"][l])
    ffn(0)
    plain(i["attn_w_q"][0])
    plain(i["w_kvf"], 0, 2 * D)
    plain(i["attn_w_o"][0])
    ffn(1)
    w = i["w_in_2"][0]
    plain(w, 5 * HALF, 6 * HALF)

    def branch(n):
        for half in range(2):
            c = 6 * HALF + n * D + half * HALF
            plain(w, c, c + HALF)
            plain(i["w_branch_2"][0, n], half * HALF, (half + 1) * HALF, rows=4)
    branch(2)
    plain(w, 0, 2 * HALF)
    plain(w, 2 * HALF, 5 * HALF)
    branch(0)
    branch(1)
    plain(i["w_out_2"][0])
    for c in range(3):
        pairs(i["w_ffn_gate_2"][0], i["w_ffn_up_2"][0], range(c * D, (c + 1) * D, P), range(c * D, (c + 1) * D, P))
        plain(i["w_ffn_down_2"][0][c * D:(c + 1) * D])
    return np.stack(out)


def _params(i):
    import numpy as np

    def cols(*vs):
        return np.concatenate([np.asarray(v).reshape(-1, P).T for v in vs], axis=1)
    b1 = i["conv_b_pw1"][0]
    slope = np.broadcast_to((2.0 ** -np.arange(1.0, 9.0)).astype(np.float32), (P, 8))
    b_f = np.zeros((P, 1), np.float32)
    b_f[0:16, 0] = i["b_f"]
    parts = {
        "mix0": cols(i["mix_norm"][0]), "mix1": cols(i["mix_norm"][1]), "b_a1": cols(b1[:D]), "b_g1": cols(b1[D:]),
        "w_dw": cols(*i["conv_w_dw"][0]), "b_dw": cols(i["conv_b_dw"][0]), "ln_g": cols(i["conv_ln_g"][0]),
        "ln_b": cols(i["conv_ln_b"][0]), "b_pw2": cols(i["conv_b_pw2"][0]), "kv": cols(i["kv_norm"]),
        "ffn0": cols(i["ffn_norm"][0]), "ffn1": cols(i["ffn_norm"][1]), "ple0": cols(i["ple_norm"][0]),
        "ple1": cols(i["ple_norm"][1]), "final1": cols(i["final_norm"]), "mix2": cols(i["mix_norm_gain_2"][0]),
        "lru_w": cols(*i["lru_conv_w_2"][0]), "lru_b": cols(i["lru_conv_b_2"][0]),
        "lru_ba": cols(i["lru_b_a_2"][0].reshape(-1)), "lru_bx": cols(i["lru_b_x_2"][0].reshape(-1)),
        "lam": cols(i["lru_lambda_2"][0]), "memg": cols(i["mem_norm_gain_2"][0]), "ffn2": cols(i["ffn_norm_gain_2"][0]),
        "cw": cols(*i["ffn_conv_w_2"][0]), "cb": cols(i["ffn_conv_b_2"][0]), "final2": cols(i["final_norm_gain_2"]),
        "slope": slope, "b_f": b_f,
    }
    return np.concatenate([parts[n] for n, _ in PARAM_BLOCKS], axis=1)


def _major(a):
    return a.reshape(a.shape[0], -1, P).transpose(2, 1, 0)


def kernel(**inputs):
    import numpy as np
    import concourse.bacc as bacc
    from concourse.bass_utils import run_bass_kernel_spmd

    i = {k: np.asarray(v) for k, v in inputs.items()}
    arrays = {
        "w": _slabs(i), "par": _params(i), "x": _major(i["x"][0]), "mem": _major(i["mem_2"][0]),
        "p": np.stack([_major(i["p"][l, 0]) for l in range(2)]),
        "wf": i["w_kvf"][:, 2 * D:].reshape(KB, P, 16).transpose(1, 0, 2),
        "w_a": i["lru_w_a_2"][0].reshape(4, 2, 64, 64), "w_x": i["lru_w_x_2"][0].reshape(4, 2, 64, 64),
    }
    arrays = {k: np.ascontiguousarray(a) for k, a in arrays.items()}
    nc = bacc.Bacc("TRN2", target_bir_lowering=False, num_devices=1)
    hbm = {k: nc.dram_tensor(k + "_hbm", a.shape, mybir.dt.from_np(a.dtype), kind="ExternalInput").ap()
           for k, a in arrays.items()}
    out = nc.dram_tensor("out_hbm", (P, KB, S), F32, kind="ExternalOutput").ap()
    build(nc, hbm, out)
    r = run_bass_kernel_spmd(nc, [{k + "_hbm": a for k, a in arrays.items()}], core_ids=[0])
    got = r.results[0]["out_hbm"]
    return np.ascontiguousarray(got.transpose(2, 1, 0).reshape(1, S, D))
```

```python
from contextlib import ExitStack

import concourse.bass as bass
from concourse import mybir

F32 = mybir.dt.float32
F32R = mybir.dt.float32r
BF16 = mybir.dt.bfloat16
ALU = mybir.AluOpType
ACT = mybir.ActivationFunctionType
AX = mybir.AxisListType

P = 128
S = 512
D = 1024
KB = D // P
QB = S // P
SLAB = 16 * P
TAPS = 31
POOL_TAPS = 9
EPS = 1e-6
MEM = 256
HALF = 512
NEG = -1e30
MID_TAP, GATE_TAP = 3, 7
OUT_TAP, U_TAP = 14, 17
TURN = 4
ATANH = [1.0 / (2 * k + 1) for k in range(1, 9)]

PARAM_BLOCKS = [
    ("mix0", 8), ("mix1", 8), ("b_a1", 8), ("b_g1", 8), ("w_dw", 8 * TAPS), ("b_dw", 8), ("ln_g", 8), ("ln_b", 8),
    ("b_pw2", 8), ("kv", 8), ("ffn0", 8), ("ffn1", 8), ("ple0", 8), ("ple1", 8), ("final1", 8),
    ("mix2", 8), ("lru_w", 16), ("lru_b", 4), ("lru_ba", 4), ("lru_bx", 4), ("lam", 4), ("memg", 8),
    ("ffn2", 8), ("cw", 24 * 3), ("cb", 24), ("final2", 8), ("slope", 8), ("b_f", 1),
]
COL, _n = {}, 0
for _name, _k in PARAM_BLOCKS:
    COL[_name] = _n
    _n += _k
NPARAM = _n


class Pos:

    def __init__(self, const, step=0, i=0):
        self.const, self.step, self.i = const, step, i

    def at(self, d=0):
        return self.const + d + self.step * self.i

    def slot(self, ring, d=0):
        return (self.const + d) % ring

    def turns(self, ring, d=0):
        assert self.step % ring == 0
        return (self.const + d) // ring + (self.step // ring) * self.i

    def plus(self, d):
        return Pos(self.const + d, self.step, self.i)


class Ledger:

    def __init__(self):
        self.count = {}

    def take(self, name, n):
        base = self.count.get(name, 0)
        self.count[name] = base + n
        return base


def build(nc, hbm, out):
    led = Ledger()

    def phase(slabs=0, blks=0, **more):
        at = {"slab": led.take("slab", slabs), "blk": led.take("blk", blks)}
        at.update({k: led.take(k, n) for k, n in more.items()})
        return at

    x0 = phase(split=8, sq=8, acc=7, norm=1, stat=1)
    p_split = [None, None]
    pw1 = phase(slabs=8, blks=16, sg=8)
    memkv = phase(slabs=4, blks=8)
    ln = phase(split=8, norm=1)
    pw2 = phase(slabs=4, blks=8, split=8, sq=8, acc=7, norm=1, stat=1)
    ffn, proj, gate = [None, None], [None, None], [None, None]

    def plan_ffn(l):
        ffn[l] = phase(slabs=32, blks=64, full=32, split=40, sq=8, acc=7, norm=1, stat=1)
        proj[l] = phase(slabs=1, blks=8)
        gate[l] = phase(slabs=4, blks=8, sg=8, gm=8, hg=8, split=8 if l == 0 else 0, sq=8, acc=7, norm=1, stat=1)

    plan_ffn(0)
    kvsplit = phase(split=8)
    gq = phase(slabs=4, blks=8)
    gk = phase(slabs=4, blks=8)
    gv = phase(slabs=4, blks=16)
    fox = phase(split=8, step=64, unit=8)
    wo = phase(slabs=4, blks=8, split=8, sq=8, acc=7, norm=1, stat=1)
    p_split[1] = phase(split=1)
    plan_ffn(1)
    fin = phase(split=8, norm=1, stat=1)
    gqx = phase(slabs=2, blks=4)
    xat = phase(split=4, step=16, unit=4)
    br = [None] * 3
    br[2] = phase(slabs=6, blks=16, sg=8)
    gxg = phase(slabs=4, blks=8)
    lru = phase(split=4)
    gqm = phase(slabs=2, blks=4)
    gkm = phase(slabs=2, blks=4)
    gvm = phase(slabs=2, blks=8)
    br[0] = phase(slabs=6, blks=16, sg=8, gm=8)
    mob = phase(split=4, step=32, unit=4)
    br[1] = phase(slabs=6, blks=16, sg=8, gm=8)
    mrg = phase(split=8)
    wout = phase(slabs=4, blks=8, split=8, sq=8, acc=7, norm=1, stat=1)
    ffn2 = phase(slabs=36, blks=72, full=24, split=24, sq=8, acc=7, norm=1, stat=1)
    NS = led.count["slab"]

    with ExitStack() as ctx:
        def sb(name, shape, dt=F32, where=ctx):
            return where.enter_context(nc.sbuf_tensor(name, shape, dt))

        def sem(name):
            return ctx.enter_context(nc.semaphore(name))

        with ExitStack() as early:
            b_hi = sb("b_hi", [P, KB, S], F32R, early)
            b_lo = sb("b_lo", [P, KB, S], F32R, early)
        kT = sb("kT", [P, KB, S])
        sb("rest_of_b", [P, KB, S])
        a_hi, a_lo = sb("a_hi", [P, KB, S], F32R), sb("a_lo", [P, KB, S], F32R)
        A, B = (a_hi, a_lo), (b_hi, b_lo)
        h = sb("h", [P, KB, S])
        raw = sb("raw", [P, 2, SLAB])
        w_hi, w_lo = sb("w_hi", [P, 2, SLAB], F32R), sb("w_lo", [P, 2, SLAB], F32R)
        par = sb("par", [P, NPARAM])
        inv_d = sb("inv_d", [P, P])
        ident, identb, tri = sb("ident", [P, P]), sb("identb", [P, P], BF16), sb("tri", [P, P], BF16)
        T = sb("T", [P, 4, S])
        U = sb("U", [P, 2, S])
        acc_sq, sqb = sb("acc_sq", [P, S]), sb("sqb", [P, 2, S])
        rstd, var = sb("rstd", [P, S]), sb("var", [P, S])
        mkv = sb("mkv", [P, 4 * S])
        mk = mkv[:, 0:4 * MEM].rearrange("p (c s) -> p c s", c=4)
        mv = mkv[:, 4 * MEM:].rearrange("p (t n) -> p t n", t=2)
        rcol, colv = sb("rcol", [P, QB]), sb("colv", [P, QB])
        nmax, rsum, rinv = sb("nmax", [P, 4]), sb("rsum", [P, 4]), sb("rinv", [P, 4])
        sp = sb("sp", [P, 8, 4])
        slope_of = sb("slope_of", [P, 2])
        fin_gain, colv2 = sb("fin_gain", [P, KB]), sb("colv2", [P, QB])
        with ExitStack() as la:
            u_pad = sb("u_pad", [P, KB, TAPS - 1 + S], F32, la)
            pool_sum = sb("pool_sum", [P, 2, S], F32, la)
            mem_raw = sb("mem_raw", [P, KB, MEM], F32, la)
            p_raw0 = sb("p_raw0", [P, 2, S], F32, la)
            p_hi0, p_lo0 = sb("p_hi0", [P, 2, S], F32R, la), sb("p_lo0", [P, 2, S], F32R, la)
        with ExitStack() as lb:
            v_s, qT = sb("v_s", [P, QB, D], F32, lb), sb("qT", [P, KB, S], F32, lb)
            with ExitStack() as lb1:
                wf = sb("wf", [P, KB, 16], F32, lb1)
                wf_hi, wf_lo = sb("wf_hi", [P, KB, P], F32R, lb1), sb("wf_lo", [P, KB, P], F32R, lb1)
            fbias = sb("fbias", [P, 2, S], F32, lb)
        with ExitStack() as lf:
            big1 = sb("big1", [P, KB, S], F32, lf)
            p_raw1 = sb("p_raw1", [P, 2, S], F32, lf)
            p_hi1, p_lo1 = sb("p_hi1", [P, 2, S], F32R, lf), sb("p_lo1", [P, 2, S], F32R, lf)
        with ExitStack() as lc:
            merged = sb("merged", [P, KB, S], F32, lc)
            with ExitStack() as c1:
                qx = sb("qx", [P, 4, S], F32, c1)
            with ExitStack() as c2:
                xap = sb("xap", [P, 4, S + 3], F32, c2)
                ga = sb("ga", [P, 4, S], F32, c2)
                xc = sb("xc", [P, 4, S], F32, c2)
                wga, wgx = sb("wga", [P, 4, P], F32, c2), sb("wgx", [P, 4, P], F32, c2)
            with ExitStack() as c3:
                qm, vm = sb("qm", [P, 4, S], F32, c3), sb("vm", [P, QB, HALF], F32, c3)
                mbias = sb("mbias", [P, 2, 7 * P], F32, c3)
                dist = sb("dist", [P, 7 * P], F32, c3)
        with ExitStack() as ld:
            gpad = sb("gpad", [P, 2, S + 2], F32, ld)
        km = mkv[:, :].rearrange("p (c s) -> p c s", c=4)
        big = u_pad[:, :, TAPS - 1:]
        bigs, p_raw, p_hi, p_lo = (big, big1), (p_raw0, p_raw1), (p_hi0, p_hi1), (p_lo0, p_lo1)
        acc_fin = p_raw1[:, 0]
        prob, probT = T, (U[:, 1, :], acc_sq)
        o_sb = U[:, 0, :].rearrange("p (t n) -> p t n", t=QB)
        qs = sqb
        dt_i = mybir.dt.int32
        mem_sq = mkv[:, :].rearrange("p (k s) -> p k s", k=KB)
        SP_OPS = 9 + len(ATANH)
        CONV_OPS = 2 * (TAPS - POOL_TAPS + 1)

        gp = ctx.enter_context(nc.psum_tensor("gp", [P, 4, S], F32))
        ms = ctx.enter_context(nc.psum_tensor("ms", [P, 4, S], F32))

        negc_hbm = nc.dram_tensor("negc_scratch", (16, S), F32, kind="Internal").ap()

        raw_ready = [sem(f"raw_ready{i}") for i in range(2)]
        w_hi_done, w_lo_done = sem("w_hi_done"), sem("w_lo_done")
        blk_done = sem("blk_done")
        evac = [sem(f"evacuated{i}") for i in range(4)]
        hi_done, lo_done = sem("hi_done"), sem("lo_done")
        x_ready = [sem(f"x_ready{i}") for i in range(4)]
        par_ready, mem_ready = sem("par_ready"), sem("mem_ready")
        p_ready, wf_ready, wg_ready = sem("p_ready"), sem("wf_ready"), sem("wg_ready")
        const_ready, wf_zero, wg_zero, pad_zero = sem("const_ready"), sem("wf_zero"), sem("wg_zero"), sem("pad_zero")
        sq_done, acc_done, stat_done, var_done, rstd_done = (
            sem("sq_done"), sem("acc_done"), sem("stat_done"), sem("var_done"), sem("rstd_done"))
        eps_done = sem("eps_done")
        col_stat, col_eps, col_var, col_done = sem("col_stat"), sem("col_eps"), sem("col_var"), sem("col_done")
        msq_done, mstat_done, mvar_done, mrstd_done, mscaled = (
            sem("msq_done"), sem("mstat_done"), sem("mvar_done"), sem("mrstd_done"), sem("mscaled"))
        meps_done = sem("meps_done")
        mp_hi, mp_lo = sem("mem_p_hi"), sem("mem_p_lo")
        tap_done, pool_conv = sem("tap_product"), sem("pool_conv")
        full = sem("full")
        sg_done = sem("sigmoid_done")
        u_done, conv_done = sem("u_done"), sem("conv_done")
        mean_done, centred, csq_done, cvar_done, normed = (
            sem("mean_done"), sem("centred"), sem("csq_done"), sem("cvar_done"), sem("normed"))
        gm_done, hg_done = sem("gated"), sem("h_gated")
        h_done = sem("h_done")
        fin_gain_done, fin_sq, fin_acc, fin_chain = sem("fin_gain"), sem("fin_sq"), sem("fin_acc"), sem("fin_chain")
        f_stat, f_v, f_exp, f_stored, f_chain = (
            sem("f_stat"), sem("f_v"), sem("f_exp"), sem("f_stored"), sem("f_chain"))
        wf_split, wf_hi_done, silu_done = sem("wf_split"), sem("wf_hi_done"), sem("silu_done")
        q_zero, q_copied, bias_ready = sem("q_zero"), sem("q_copied"), [sem(f"bias_ready{i}") for i in range(2)]
        scored, biased, exped, transposed, pt_copied, pv_done, o_done, ot_done, sum_inv = (
            sem("scored"), sem("biased"), sem("exped"), sem("transposed"), sem("pt_copied"), sem("pv_done"),
            sem("o_done"), sem("ot_done"), sem("sum_inv"))
        xa_c, l_gate, l_act, l_chain, l_y = (
            sem("xa_conv"), sem("lru_gate_mm"), sem("lru_act"), sem("lru_chain"), sem("lru_y"))
        step_open = sem("step_open")
        sp_e, sp_chain = sem("sp_exp"), sem("sp_chain")
        g_chain, gelu_done = sem("g_chain"), sem("gelu_done")
        dist_ready, slope_copied, mb_ready = sem("dist_ready"), sem("slope_copied"), sem("mb_ready")
        out_ready, stored = sem("out_ready"), sem("stored")

        def col(name, k, n=1):
            return par[:, COL[name] + k:COL[name] + k + n]

        def u_of(k, t):
            return u_pad[:, k, t:t + S] if isinstance(k, int) else u_pad[:, bass.ds(k, 1), t:t + S].rearrange("p a s -> p (a s)")

        def f32(ap):
            return ap.bitcast(F32)

        block = ctx.enter_context(nc.Block())

        @block.sync
        def _(q):

            def slab(pos, first):
                s = pos.slot(2)
                if not first:
                    q.wait_ge(w_lo_done, pos.at(-1))
                q.dma_start(raw[:, s], hbm["w"][pos.at()] if isinstance(pos.at(), int)
                            else hbm["w"][bass.ds(pos.at(), 1)].rearrange("a p n -> p (a n)")
                            ).then_inc(raw_ready[s], 16)

            def slabs(a, b):
                while a < 2:
                    slab(Pos(a), True)
                    a += 1
                if (b - a) % 2:
                    slab(Pos(a), False)
                    a += 1
                if b > a:
                    with q.Fori(0, (b - a) // 2) as i:
                        slab(Pos(a, 2, i), False)
                        slab(Pos(a + 1, 2, i), False)

            slab(Pos(0), True)
            q.dma_start(par[:], hbm["par"]).then_inc(par_ready, 16)
            for c in range(4):
                q.dma_start(h[:, 2 * c:2 * c + 2], hbm["x"][:, 2 * c:2 * c + 2]).then_inc(x_ready[c], 16)
            slab(Pos(1), True)
            q.dma_start(mem_raw[:], hbm["mem"]).then_inc(mem_ready, 16)
            q.dma_start(p_raw0[:], hbm["p"][0]).then_inc(p_ready, 16)
            slabs(2, gk["slab"])
            q.wait_ge(hg_done, gate[0]["hg"] + 8)
            q.dma_start(wf[:], hbm["wf"]).then_inc(wf_ready, 16)
            slabs(gk["slab"], gv["slab"] + 2)
            q.wait_ge(f_v, 3)
            q.dma_start(negc_hbm, T[0:16, 3]).then_inc(f_stored, 16)
            q.wait_ge(f_stored, 16)

            def fox_bias(j, hh, first):
                if not first:
                    q.wait_ge(biased, 8 * j - 8 + 4 * (hh + 1))
                q.dma_start(fbias[:, hh], negc_row(2 * j + hh)).then_inc(bias_ready[hh], 16)

            def negc_row(r):
                src = negc_hbm[bass.ds(r, 1), :] if not isinstance(r, int) else negc_hbm[r:r + 1, :]
                return src.broadcast_to([P, S])
            fox_bias(0, 0, True)
            fox_bias(0, 1, True)
            slabs(gv["slab"] + 2, wo["slab"] + 2)
            with q.Fori(1, 8) as j:
                fox_bias(j, 0, False)
                fox_bias(j, 1, False)
            q.wait_ge(lo_done, fox["split"] + 8)
            q.dma_start(p_raw1[:], hbm["p"][1]).then_inc(p_ready, 16)
            slabs(wo["slab"] + 2, gxg["slab"])
            for t, name in ((wga, "w_a"), (wgx, "w_x")):
                q.wait_ge(wg_zero, 2)
                for hh in range(2):
                    q.dma_start(t[64 * hh:64 * hh + 64, :, 64 * hh:64 * hh + 64],
                                hbm[name][:, hh].rearrange("j i o -> i j o")).then_inc(wg_ready, 16)
            slabs(gxg["slab"], NS)
            o_v = out
            for c in range(4):
                q.wait_ge(out_ready, 2 * (c + 1))
                q.dma_start(o_v[:, 2 * c:2 * c + 2], h[:, 2 * c:2 * c + 2]).then_inc(stored, 16)
            q.wait_ge(stored, 64)

        @block.gpsimd
        def _(g):
            g.memset(ident[:], 0.0).then_inc(const_ready, 1)
            g.memset(identb[:], 0.0).then_inc(const_ready, 1)
            g.memset(tri[:], 0.0).then_inc(const_ready, 1)
            g.memset(inv_d[:], 1.0 / D).then_inc(const_ready, 1)
            g.memset(u_pad[:, :, 0:TAPS - 1], 0.0).then_inc(pad_zero, 1)
            g.wait_ge(const_ready, 4)
            for m in (ident, identb):
                g.affine_select(out=m[:], in_=m[:], compare_op=ALU.not_equal, fill=1.0, base=0,
                                pattern=[[-1, P]], channel_multiplier=1).then_inc(const_ready, 1)
            g.affine_select(out=tri[:], in_=tri[:], compare_op=ALU.is_ge, fill=NEG, base=0,
                            pattern=[[-1, P]], channel_multiplier=1).then_inc(const_ready, 1)

            def slab(pos):
                s = pos.slot(2)
                g.wait_ge(w_hi_done, pos.at(1))
                g.tensor_tensor(w_lo[:, s], raw[:, s], f32(w_hi[:, s]), ALU.subtract).then_inc(w_lo_done, 1)

            def slabs(a, b):
                if (b - a) % 2:
                    slab(Pos(a))
                    a += 1
                if b > a:
                    with g.Fori(0, (b - a) // 2) as i:
                        slab(Pos(a, 2, i))
                        slab(Pos(a + 1, 2, i))

            def copies(q_of, at, n, base, next_slab, bias=None):
                def one(j, first):
                    for hh in range(2):
                        lo, hi = 64 * hh, 64 * hh + 64
                        if not first:
                            g.wait_ge(scored, at["step"] + 8 * j - 8 + 4 * (hh + 1))
                        if not (first and hh == 0):
                            g.wait_ge(q_copied, base + 2 * j + hh)
                            if bias:
                                g.wait_ge(mb_ready, 2 * j + hh)
                        g.tensor_copy(qs[lo:hi, hh], q_of(lo, hi, j)).then_inc(q_copied, 1)
                        if bias:
                            if not first:
                                g.wait_ge(biased, at["step"] + 8 * j - 8 + 4 * (hh + 1))
                            g.wait_ge(q_copied, base + 2 * j + hh + 1)
                            bias(j, hh)
                g.wait_ge(w_lo_done, next_slab)
                g.memset(qs[:, 0], 0.0).then_inc(q_zero, 1)
                g.memset(qs[:, 1], 0.0).then_inc(q_zero, 1)
                g.wait_ge(q_zero, base // 8 + 2)
                one(0, True)
                g.wait_ge(q_copied, base + 2)
                if bias:
                    g.wait_ge(mb_ready, 2)
                slab(Pos(next_slab))
                g.wait_ge(w_lo_done, next_slab + 1)
                with g.Fori(1, n) as j:
                    one(j, False)
                g.wait_ge(q_copied, base + 2 * n)

            def dyn(t):
                return lambda lo, hi, j: t[lo:hi, j, :] if isinstance(j, int) else t[lo:hi, bass.ds(j, 1), :].rearrange("p a s -> p (a s)")

            def add_taps(i, extra=True):
                for t in range(1, POOL_TAPS):
                    for s in range(2):
                        g.wait_ge(tap_done, 2 * POOL_TAPS * i + 2 * t + s + 1)
                        if t >= 2:
                            g.wait_ge(pool_conv, 2 * (POOL_TAPS - 1) * i + 2 * t + s - 3)
                        g.tensor_tensor(pool_sum[:, s], pool_sum[:, s], sqb[:, s], ALU.add).then_inc(pool_conv, 1)
                    if t == MID_TAP + 2:
                        slab(Pos(4, 2, i))
                if extra:
                    slab(Pos(5, 2, i))

            slabs(0, 4)
            add_taps(0)
            with g.Fori(1, 3) as i:
                add_taps(i)
            g.wait_ge(mp_hi, 1)
            g.tensor_tensor(b_lo[:, :, 0:MEM], mem_raw[:], f32(b_hi[:, :, 0:MEM]), ALU.subtract).then_inc(mp_lo, 1)
            add_taps(3, extra=False)
            g.wait_ge(mp_hi, 2)
            g.tensor_tensor(p_lo0[:], p_raw0[:], f32(p_hi0[:]), ALU.subtract).then_inc(mp_lo, 1)
            slabs(11, gq["slab"] + 1)
            g.wait_ge(hg_done, gate[0]["hg"] + 8)
            g.memset(f32(wf_hi[:]), 0.0).then_inc(wf_zero, 1)
            g.memset(f32(wf_lo[:]), 0.0).then_inc(wf_zero, 1)
            slabs(gq["slab"] + 1, wo["slab"])
            g.wait_ge(f_stored, 16)
            copies(dyn(qT), fox, 8, 0, wo["slab"])
            slabs(wo["slab"] + 1, gxg["slab"])
            g.wait_ge(lo_done, xat["split"] + 4)
            g.memset(wga[:], 0.0).then_inc(wg_zero, 1)
            g.memset(wgx[:], 0.0).then_inc(wg_zero, 1)
            g.memset(xap[:, :, 0:3], 0.0).then_inc(pad_zero, 1)
            slabs(gxg["slab"], br[1]["slab"])
            g.wait_ge(lo_done, lru["split"] + 4)
            g.iota(dist[:].bitcast(dt_i), pattern=[[1, 7 * P]], base=-3 * P, channel_multiplier=-1).then_inc(dist_ready, 1)
            g.wait_ge(dist_ready, 1)
            g.tensor_copy(dist[:], dist[:].bitcast(dt_i)).then_inc(dist_ready, 1)
            last = gvm["blk"] + 7
            g.wait_ge(evac[3], last // 4 + 1)

            def mob_bias(j, hh):
                sl = col("slope", 2 * j + hh) if isinstance(j, int) else par[:, bass.ds(COL["slope"] + 2 * j + hh, 1)]
                g.tensor_copy(slope_of[:, hh:hh + 1], sl).then_inc(slope_copied, 1)
                g.wait_ge(slope_copied, 2 * j + hh + 1)
                g.tensor_tensor(mbias[:, hh], dist[:], slope_of[:, hh:hh + 1].broadcast_to([P, 7 * P]), ALU.mult
                                ).then_inc(mb_ready, 1)
            g.wait_ge(dist_ready, 2)
            copies(dyn(qm), mob, 4, 16, br[1]["slab"], mob_bias)
            slabs(br[1]["slab"] + 1, ffn2["slab"])
            g.wait_ge(lo_done, mrg["split"] + 8)
            g.memset(gpad[:, :, 0:2], 0.0).then_inc(pad_zero, 1)
            slabs(ffn2["slab"], NS)

        def wait_blk(eng, pos, c):
            eng.wait_ge(blk_done, pos.at(c + 1))

        def wait_evac(eng, pos, c):
            eng.wait_ge(evac[pos.slot(4, c)], pos.turns(4, c) + 1)

        @block.tensor
        def _(pe):
            def free_bank(pos, c):
                b = pos.slot(4, c)
                if pos.const + c >= 4:
                    pe.wait_ge(evac[b], pos.turns(4, c))
                return b

            def three(o, wh, wl, xh, xl, start, stop):
                pe.matmul(o, wh, xh, start=start, stop=False)
                pe.matmul(o, wh, xl, start=False, stop=False)
                return pe.matmul(o, wl, xh, start=False, stop=stop)

            def slab_ws(sp_, bp, x, k0=0, kk=8, n=S, ready=None, hook=None):
                s = sp_.slot(2)
                cc = 16 // kk
                pe.wait_ge(w_lo_done, sp_.at(1))
                for c in range(cc):
                    b = free_bank(bp, c)
                    for k in range(kk):
                        if ready is not None and c == 0:
                            pe.wait_ge(lo_done, ready.at(k + 1))
                        at = (k * cc + c) * P
                        m = three(gp[:, b, 0:n], w_hi[:, s, at:at + P], w_lo[:, s, at:at + P],
                                  x[0][:, k0 + k, 0:n], x[1][:, k0 + k, 0:n], k == 0, k == kk - 1)
                    m.then_inc(blk_done, 1)
                    if hook and c == 0:
                        hook()

            def slab_xs(sp_, bp, x, tiles):
                s = sp_.slot(2)
                pe.wait_ge(w_lo_done, sp_.at(1))
                for t in range(tiles):
                    b = free_bank(bp, t)
                    for k in range(8):
                        xh, xl = x[0][:, k, t * P:t * P + P], x[1][:, k, t * P:t * P + P]
                        wh, wl = w_hi[:, s, k * 256:k * 256 + 256], w_lo[:, s, k * 256:k * 256 + 256]
                        m = three(gp[:, b, 0:256], xh, xl, wh, wl, k == 0, k == 7)
                    m.then_inc(blk_done, 1)

            def gemm(at, x, n_slabs=4, hook=None, ready=None, off=0, boff=None, **kw):
                boff = 2 * off if boff is None else boff
                a = 0
                if hook or ready is not None:
                    for a in range(2):
                        slab_ws(Pos(at["slab"] + off + a), Pos(at["blk"] + boff + 2 * a), x,
                                ready=Pos(ready) if a == 0 else None, hook=hook if a == 0 else None, **kw)
                    a = 2
                if n_slabs > a:
                    if n_slabs - a == 2:
                        for s in range(2):
                            slab_ws(Pos(at["slab"] + off + a + s), Pos(at["blk"] + boff + 2 * (a + s)), x, **kw)
                    else:
                        with pe.Fori(0, (n_slabs - a) // 2) as i:
                            for s in range(2):
                                slab_ws(Pos(at["slab"] + off + a + s, 2, i), Pos(at["blk"] + boff + 2 * (a + s), 4, i), x, **kw)

            def stat(at, src_ready):
                pe.wait_ge(acc_done, src_ready)
                pe.matmul(ms[:, 0, :], inv_d[:], acc_sq[:], start=True, stop=True).then_inc(stat_done, 1)

            def col_stats():
                for t in range(QB):
                    m = pe.matmul(ms[:, 1, t:t + 1], acc_sq[:, t * P:t * P + P], inv_d[:, 0:1],
                                  start=True, stop=True, skip_group_check=True)
                m.then_inc(col_stat, 1)

            pe.wait_ge(const_ready, 7)
            def memory_stat():
                pe.wait_ge(msq_done, 1)
                for k in range(8):
                    m = pe.matmul(ms[:, 1, 0:MEM], inv_d[:], mem_sq[:, k], start=(k == 0), stop=(k == 7))
                m.then_inc(mstat_done, 1)
            for s in range(2):
                slab_ws(Pos(s), Pos(2 * s), A, ready=Pos(x0["split"]) if s == 0 else None,
                        hook=memory_stat if s else lambda: stat(x0, x0["acc"] + 7))
            with pe.Fori(0, 3) as i:
                for s in range(2):
                    slab_ws(Pos(2 + s, 2, i), Pos(4 + 2 * s, 4, i), A)
            pe.wait_ge(mp_lo, 1)
            for s in range(2):
                slab_ws(Pos(memkv["slab"] + s), Pos(memkv["blk"] + 2 * s), B, n=MEM)
            for k in range(8):
                pe.wait_ge(conv_done, CONV_OPS * (k // 2 + 1))
                m = pe.matmul(ms[:, 1, :], inv_d[:], big[:, k], start=(k == 0), stop=(k == 7))
            m.then_inc(mean_done, 1)
            slab_xs(Pos(memkv["slab"] + 2), Pos(memkv["blk"] + 4), B, 2)
            for k in range(8):
                pe.wait_ge(csq_done, k + 1)
                pe.matmul(ms[:, 2, :], inv_d[:], sqb[:, k % 2], start=(k == 0), stop=(k == 7)).then_inc(cvar_done, 1)
            slab_xs(Pos(memkv["slab"] + 3), Pos(memkv["blk"] + 6), B, 2)
            gemm(pw2, B, ready=ln["split"])

            def ffn_layer(l, X, H_):
                f = ffn[l]
                src = pw2 if l == 0 else wo
                gemm(f, X, ready=src["split"], hook=lambda: stat(f, src["acc"] + 7))
                with pe.Fori(0, 3) as i:
                    for s in range(8):
                        down = s < 4
                        slab_ws(Pos(f["slab"] + 4 + s, 8, i), Pos(f["blk"] + 8 + 2 * s, 16, i),
                                H_ if down else X, ready=Pos(f["split"], 8, i) if s == 0 else None)
                for s in range(4):
                    slab_ws(Pos(f["slab"] + 28 + s), Pos(f["blk"] + 56 + 2 * s), H_, ready=Pos(f["split"] + 24) if s == 0 else None)
                if l == 0:
                    pe.wait_ge(mp_lo, 2)
                else:
                    pe.wait_ge(lo_done, p_split[l]["split"] + 1)
                slab_ws(Pos(proj[l]["slab"]), Pos(proj[l]["blk"]), (p_hi[l], p_lo[l]), kk=2)
                gemm(gate[l], X, ready=f["split"] + 32, hook=lambda: stat(gate[l], f["acc"] + 7))

            ffn_layer(0, A, B)

            def kv_stats():
                stat(gq, gate[0]["acc"] + 7)
                col_stats()
            gemm(gq, B, ready=gate[0]["split"], hook=kv_stats)
            pe.wait_ge(lo_done, kvsplit["split"] + 8)
            pe.wait_ge(wf_split, 1)
            for k in range(8):
                m = three(ms[:, 2, :], wf_hi[:, k], wf_lo[:, k], a_hi[:, k], a_lo[:, k], k == 0, k == 7)
            m.then_inc(f_stat, 1)
            gemm(gk, A)
            with pe.Fori(0, 2) as i:
                for s in range(2):
                    slab_xs(Pos(gv["slab"] + s, 2, i), Pos(gv["blk"] + 4 * s, 8, i), A, 4)

            def attention(at, n, s_read, n_of, scores, v_of, vw, before_unit, looped):
                t0, per = at["step"], len(n_of)
                turn = min(TURN, per - 1)

                def T_(pos, s):
                    pe.wait_ge(exped, pos.at(s + 1))
                    if pos.const + s - t0 >= 2 or pos.step:
                        pe.wait_ge(pt_copied, pos.at(s - 1))
                    for kb in range(n_of[s % per]):
                        m = pe.transpose(ms[:, 2 + s % 2, kb * P:kb * P + P], prob[:, s % 4, kb * P:kb * P + P], ident[:])
                    m.then_inc(transposed, 1)

                def S_(pos, j, s, first):
                    if before_unit:
                        before_unit(j, s)
                    if not (first and s < 2):
                        pe.wait_ge(s_read, pos.at(s - 1))
                    scores(j, s).then_inc(scored, 1)

                def V_(pos, j, s):
                    pe.wait_ge(pt_copied, pos.at(s + 1))
                    if pos.const + s - t0 >= 2 or pos.step:
                        pe.wait_ge(o_done, pos.at(s - 1))
                    for kb in range(n_of[s % per]):
                        m = pe.matmul(gp[:, s % 2, 0:vw], probT[s % 2][:, kb * P:kb * P + P], v_of(j, s % per, kb),
                                      start=(kb == 0), stop=(kb == n_of[s % per] - 1))
                    m.then_inc(pv_done, 1)

                def O_(pos, j, up):
                    pe.wait_ge(o_done, pos.at(per))
                    if not isinstance(j, int) or j > 0:
                        pe.wait_ge(lo_done, up)
                    for t in range(QB):
                        m = pe.transpose(gp[:, 2, t * P:t * P + P], o_sb[:, t, :], ident[:])
                    m.then_inc(ot_done, 1)

                def unit(pos, j, first):
                    prev = Pos(pos.const - per, pos.step, pos.i)
                    for s in range(per):
                        S_(pos, j, s, first)
                        if s >= 2:
                            T_(pos, s - 2)
                        elif not first:
                            T_(prev, per - 2 + s)
                        if s >= 3:
                            V_(pos, j, s - 3)
                        elif not first:
                            V_(prev, j - 1, per - 3 + s)
                        if s == turn and not first:
                            O_(prev, j - 1, at["split"] + j - 1)

                unit(Pos(t0), 0, True)
                if looped:
                    with pe.Fori(1, n) as j:
                        unit(Pos(t0, per, j), j, False)
                else:
                    for j in range(1, n):
                        unit(Pos(t0 + per * j), j, False)
                end = Pos(t0 + per * (n - 1))
                T_(end, per - 2)
                V_(end, n - 1, per - 3)
                T_(end, per - 1)
                V_(end, n - 1, per - 2)
                V_(end, n - 1, per - 1)
                O_(end, n - 1, at["split"] + n - 1)
                pe.wait_ge(lo_done, at["split"] + n)

            def head_scores(keys):
                def scores(j, s):
                    hh, qb = s // 4, s % 4
                    w = (qb + 1) * P
                    k = keys[:, j, 0:w] if isinstance(j, int) else keys[:, bass.ds(j, 1), 0:w].rearrange("p a s -> p (a s)")
                    pe.matmul(ms[:, s % 2, 0:w], qs[:, hh, qb * P:qb * P + P], k, start=True, stop=False)
                    return pe.matmul(ms[:, s % 2, qb * P:w], identb[:], tri[:], start=False, stop=True)
                return scores

            def head_v(t):
                def v_of(j, s, kb):
                    if isinstance(j, int):
                        return t[:, kb, j * P + 64 * (s // 4):j * P + 64 * (s // 4) + 64]
                    return t[:, kb, bass.ds(j * P + 64 * (s // 4), 64)]
                return v_of

            def wait_copies(base):
                def before(j, s):
                    if s in (0, 4):
                        pe.wait_ge(q_copied, base + 2 * j + s // 4 + 1)
                return before

            attention(fox, 8, biased, [1, 2, 3, 4] * 2, head_scores(kT), head_v(v_s), 64, wait_copies(0), True)
            gemm(wo, A, ready=fox["split"])
            ffn_layer(1, B, A)

            def c_stats():
                stat(gqx, gate[1]["acc"] + 7)
                pe.wait_ge(fin_acc, 7)
                pe.matmul(ms[:, 2, :], inv_d[:], acc_fin, start=True, stop=True).then_inc(stat_done, 1)
                for n, sums in enumerate((acc_sq[:], acc_fin)):
                    for t in range(QB):
                        m = pe.matmul(ms[:, 1, QB * n + t:QB * n + t + 1], sums[:, t * P:t * P + P], inv_d[:, 0:1],
                                      start=True, stop=True, skip_group_check=True)
                m.then_inc(col_stat, 1)
            gemm(gqx, A, n_slabs=2, ready=fin["split"], hook=c_stats)
            for c in range(4):
                wait_evac(pe, Pos(gqx["blk"]), c)

            def x_scores(j, s):
                return pe.matmul(ms[:, s % 2, 0:MEM], qx[:, j, s * P:s * P + P], mk[:, j, :], start=True, stop=True)
            attention(xat, 4, exped, [2] * 4, x_scores, lambda j, s, kb: mv[:, kb, j * P:j * P + P], P, None, False)

            def branch(n, k0, ysplit, kn):
                at = br[n]
                for half in range(2):
                    sl, bl = at["slab"] + 3 * half, at["blk"] + 8 * half
                    for s in range(2):
                        slab_ws(Pos(sl + s), Pos(bl + 2 * s), A)
                    pe.wait_ge(lo_done, ysplit + kn)
                    slab_ws(Pos(sl + 2), Pos(bl + 4), B, k0=k0, kk=4)

            branch(2, 4, xat["split"], 4)
            gemm(gxg, A)
            pe.wait_ge(wg_ready, 64)
            for j, (at, s) in enumerate(((gqm, 0), (gqm, 1), (gkm, 0), (gkm, 1))):
                pe.wait_ge(xa_c, 4 * (j + 1))
                if j:
                    pe.wait_ge(l_act, 4 * j - 2)
                pe.matmul(ms[:, 0, :], wga[:, j], xc[:, j], start=True, stop=True).then_inc(l_gate, 1)
                pe.matmul(ms[:, 1, :], wgx[:, j], xc[:, j], start=True, stop=True).then_inc(l_gate, 1)
                slab_ws(Pos(at["slab"] + s), Pos(at["blk"] + 2 * s), A)
            for s in range(2):
                slab_xs(Pos(gvm["slab"] + s), Pos(gvm["blk"] + 4 * s), A, 4)
            branch(0, 0, lru["split"], 4)
            for c in range(4):
                wait_evac(pe, Pos(br[0]["blk"] + 12), c)
            attention(mob, 4, biased, [1, 2, 3, 4] * 2, head_scores(km), head_v(vm), 64, wait_copies(16), True)
            branch(1, 4, mob["split"], 4)
            gemm(wout, A, ready=mrg["split"])
            f = ffn2
            src = wout
            gemm(f, B, n_slabs=2, ready=src["split"], hook=lambda: stat(f, src["acc"] + 7))
            with pe.Fori(0, 3) as i:
                for s in range(2):
                    slab_ws(Pos(f["slab"] + 2 + s, 2, i), Pos(f["blk"] + 4 + 2 * s, 4, i), B)
            with pe.Fori(0, 2) as i:
                for s in range(12):
                    slab_ws(Pos(f["slab"] + 8 + s, 12, i), Pos(f["blk"] + 16 + 2 * s, 24, i),
                            A if s < 4 else B, ready=Pos(f["split"], 8, i) if s == 0 else None)
            for s in range(4):
                slab_ws(Pos(f["slab"] + 32 + s), Pos(f["blk"] + 64 + 2 * s), A, ready=Pos(f["split"] + 16) if s == 0 else None)
            stat(None, f["acc"] + 7)

        @block.scalar
        def _(act):
            def next_w(sp_, bp):
                if not sp_.step and sp_.const + 1 >= NS:
                    return
                s = sp_.slot(2, 1)
                act.wait_ge(raw_ready[s], 16 * (sp_.turns(2, 1) + 1))
                if bp.const > 0:
                    act.wait_ge(blk_done, bp.at())
                act.activation(w_hi[:, s], raw[:, s], ACT.Copy).then_inc(w_hi_done, 1)

            def next_of(at, s, bs=None):
                next_w(Pos(at["slab"] + s), Pos(at["blk"] + (2 * s if bs is None else bs)))

            def square(c, at):
                if c >= 3:
                    act.wait_ge(acc_done, at["acc"] + c - 2)
                dst = acc_sq[:] if c == 0 else sqb[:, c % 2]
                act.activation(dst, h[:, c], ACT.Square).then_inc(sq_done, 1)

            def prep(c, X, gain, at, ready):
                ready()
                square(c, at)
                act.activation(X[0][:, c], h[:, c], ACT.Copy, scale=col(gain, c)).then_inc(hi_done, 1)

            def finish_norm(at):
                act.wait_ge(var_done, at["norm"] + 1)
                act.activation(rstd[:], var[:], ACT.Sqrt).then_inc(rstd_done, 1)

            def finish_col(n):
                act.wait_ge(col_var, n + 1)
                act.activation(rcol[:], colv[:], ACT.Sqrt).then_inc(col_done, 1)

            act.wait_ge(raw_ready[0], 16)
            act.activation(w_hi[:, 0], raw[:, 0], ACT.Copy).then_inc(w_hi_done, 1)
            act.wait_ge(par_ready, 16)
            for c in range(8):
                prep(c, A, "mix0", x0, lambda: act.wait_ge(x_ready[c // 2], 16))
            next_w(Pos(0), Pos(0))
            finish_norm(x0)
            act.wait_ge(mem_ready, 16)
            act.activation(mem_sq, mem_raw[:], ACT.Square).then_inc(msq_done, 1)

            def pw1_gates(bp, pcol):
                for s in range(2):
                    wait_evac(act, bp, 2 * s + 1)
                    act.activation(T[:, 2 * s + 1], T[:, 2 * s + 1], ACT.Sigmoid, bias=pcol("b_g1", s, 0)).then_inc(sg_done, 1)

            def tap_products(i, pcol, at_mid, at_gates):
                for t in range(POOL_TAPS):
                    for s in range(2):
                        src = u_of(2 * i + s, t)
                        if t == 0:
                            act.wait_ge(u_done, 2 * i + s + 1)
                            if not isinstance(i, int) or i:
                                act.wait_ge(conv_done, CONV_OPS * i)
                            m = act.activation(pool_sum[:, s], src, ACT.Identity, scale=pcol("w_dw", s, 0), bias=pcol("b_dw", s, 0))
                        else:
                            if t >= 2:
                                act.wait_ge(pool_conv, 2 * (POOL_TAPS - 1) * i + 2 * t + s - 3)
                            m = act.activation(sqb[:, s], src, ACT.Copy, scale=pcol("w_dw", s, 8 * t))
                        m.then_inc(tap_done, 1)
                    if t == MID_TAP:
                        at_mid()
                    if t == GATE_TAP:
                        at_gates()

            def colp(i):
                if isinstance(i, int):
                    return lambda n, s, o: col(n, o + s + 2 * i)
                return lambda n, s, o: par[:, bass.ds(COL[n] + o + s + 2 * i, 1)]

            def next_gates(i):
                pw1_gates(Pos(4, 4, i), lambda n, s, o: colp(i)(n, s, o + 2))
                next_w(Pos(4, 2, i), Pos(8, 4, i))

            def memory_rstd():
                act.wait_ge(mvar_done, 1)
                act.activation(U[:, 0, 0:MEM], var[:, 0:MEM], ACT.Sqrt).then_inc(mrstd_done, 1)
                next_w(Pos(3), Pos(6))
            next_w(Pos(1), Pos(2))
            pw1_gates(Pos(0), colp(0))
            next_w(Pos(2), Pos(4))
            tap_products(0, colp(0), memory_rstd, lambda: next_gates(0))
            act.wait_ge(mscaled, 8)
            act.activation(b_hi[:, :, 0:MEM], mem_raw[:], ACT.Copy).then_inc(mp_hi, 1)
            act.wait_ge(p_ready, 16)
            act.activation(p_hi0[:], p_raw0[:], ACT.Copy).then_inc(mp_hi, 1)
            with act.Fori(1, 3) as i:
                tap_products(i, colp(i), lambda: next_w(Pos(3, 2, i), Pos(6, 4, i)), lambda: next_gates(i))
            tap_products(3, colp(3), lambda: next_w(Pos(9), Pos(18)), lambda: None)
            for c in range(4):
                bp = Pos(memkv["blk"])
                wait_blk(act, bp, c)
                act.activation(mk[:, c, :], gp[:, bp.slot(4, c), 0:MEM], ACT.Copy).then_inc(evac[bp.slot(4, c)], 1)

            def memory_values(s):
                for t in range(2):
                    bp = Pos(memkv["blk"] + 4 + 2 * s)
                    wait_blk(act, bp, t)
                    act.activation(mv[:, t, 256 * s:256 * s + 256], gp[:, bp.slot(4, t), 0:256], ACT.Copy).then_inc(evac[bp.slot(4, t)], 1)
            next_of(memkv, 2)
            for k in range(8):
                act.wait_ge(centred, k + 1)
                if k >= 2:
                    act.wait_ge(cvar_done, k - 1)
                act.activation(sqb[:, k % 2], big[:, k], ACT.Square).then_inc(csq_done, 1)
            memory_values(0)
            next_of(memkv, 3)
            finish_norm(ln)
            memory_values(1)
            for k in range(8):
                act.wait_ge(normed, k + 1)
                if k >= 2:
                    act.wait_ge(lo_done, ln["split"] + k - 1)
                act.activation(U[:, k % 2], big[:, k], ACT.Silu, bias=col("ln_b", k), scale=col("ln_g", k)).then_inc(silu_done, 1)
                act.wait_ge(silu_done, k + 1)
                act.activation(b_hi[:, k], U[:, k % 2], ACT.Copy).then_inc(hi_done, 1)

            def add_and_prep(at, X, gain, split_at=None, bp0=None):
                for s in range(4):
                    next_of(at, s)
                    for c in range(2):
                        k = 2 * s + c
                        prep(k, X, gain, at, lambda: wait_evac(act, Pos(at["blk"]), k))
            add_and_prep(pw2, A, "ffn0")

            def up_hi(f, sp_, bp, fu, H_, k):
                next_w(sp_, bp)
                for c in range(2):
                    act.wait_ge(full, fu.at(k + c + 1))
                    act.activation(H_[0][:, k + c], U[:, (k + c) % 2], ACT.Copy).then_inc(hi_done, 1)

            def last_norm_parts(c):
                if c == 0:
                    act.wait_ge(fin_gain_done, 1)
                if c >= 3:
                    act.wait_ge(fin_acc, c - 2)
                dst = acc_fin if c == 0 else U[:, c % 2]
                act.activation(dst, h[:, c], ACT.Square, scale=col("final1", c)).then_inc(fin_sq, 1)
                act.activation(a_hi[:, c], h[:, c], ACT.Copy, scale=fin_gain[:, c:c + 1]).then_inc(hi_done, 1)

            def ffn_layer(l, X, H_):
                f = ffn[l]
                fu = f["full"]
                for s in range(4):
                    sp_, bp = Pos(f["slab"] + s), Pos(f["blk"] + 2 * s)
                    if s == 0:
                        next_w(sp_, bp)
                        finish_norm(pw2 if l == 0 else wo)
                        for c in range(2):
                            act.wait_ge(full, fu + c + 1)
                            act.activation(H_[0][:, c], U[:, c % 2], ACT.Copy).then_inc(hi_done, 1)
                    else:
                        up_hi(f, sp_, bp, Pos(fu), H_, 2 * s)
                with act.Fori(0, 3) as i:
                    for s in range(4):
                        next_w(Pos(f["slab"] + 4 + s, 8, i), Pos(f["blk"] + 8 + 2 * s, 16, i))
                    for s in range(4):
                        up_hi(f, Pos(f["slab"] + 8 + s, 8, i), Pos(f["blk"] + 16 + 2 * s, 16, i), Pos(fu + 8, 8, i), H_, 2 * s)
                for s in range(4):
                    next_of(f, 28 + s)
                    for c in range(2):
                        k = 2 * s + c
                        prep(k, X, "ple%d" % l, f, lambda: wait_evac(act, Pos(f["blk"] + 56), k))
                next_of(proj[l], 0)
                for c in range(8):
                    bp = Pos(proj[l]["blk"])
                    wait_blk(act, bp, c)
                    act.activation(bigs[l][:, c], gp[:, bp.slot(4, c)], ACT.Copy).then_inc(evac[bp.slot(4, c)], 1)
                g = gate[l]
                for c in range(9):
                    if c < 8:
                        if c % 2 == 0:
                            next_of(g, c // 2)
                        if c == 0:
                            finish_norm(f)
                        wait_evac(act, Pos(g["blk"]), c)
                        act.activation(T[:, c % 2], T[:, c % 2], ACT.Sigmoid).then_inc(sg_done, 1)
                    if c >= 1:
                        act.wait_ge(hg_done, g["hg"] + c)
                        if l == 0:
                            prep(c - 1, B, "mix1", g, lambda: None)
                        else:
                            square(c - 1, g)
                            last_norm_parts(c - 1)
            ffn_layer(0, A, B)

            act.wait_ge(blk_done, gate[0]["blk"] + 8)
            for s in range(4):
                next_of(gq, s)
                if s == 0:
                    finish_norm(gate[0])
                    finish_col(0)
                for k in range(3 * s, min(3 * s + 3, 8)):
                    act.activation(a_hi[:, k], h[:, k], ACT.Copy, scale=col("kv", k)).then_inc(hi_done, 1)
                if s == 2:
                    act.wait_ge(wf_ready, 16)
                    act.wait_ge(wf_zero, 2)
                    act.activation(wf_hi[:, :, 0:16], wf[:], ACT.Copy).then_inc(wf_hi_done, 1)
            for s in range(4):
                next_of(gk, s)
                if s == 0:
                    act.wait_ge(f_v, 2)
                    act.activation(T[0:16, 2], T[0:16, 1], ACT.Exp, scale=-1.0).then_inc(f_exp, 1)
            for s in range(4):
                next_of(gv, s, 4 * s)

            def attention(at, X, k0, n, per, looped, exp, pt_w):
                t0, turn = at["step"], min(TURN, per - 1)

                def E_(pos, s, fresh):
                    act.wait_ge(biased, pos.at(s + 1))
                    if not fresh:
                        act.wait_ge(o_done, pos.at(s - 3))
                    exp(s).then_inc(exped, 1)

                def C_(pos, s, fresh):
                    w = pt_w[s % per]
                    act.wait_ge(transposed, pos.at(s + 1))
                    if not fresh:
                        act.wait_ge(pv_done, pos.at(s - 1))
                    act.activation(probT[s % 2][:, 0:w], ms[:, 2 + s % 2, 0:w], ACT.Copy).then_inc(pt_copied, 1)

                def H_(j):
                    act.wait_ge(ot_done, at["unit"] + j + 1)
                    dst = X[0][:, k0 + j] if isinstance(j, int) else X[0][:, bass.ds(k0 + j, 1)].rearrange("p a s -> p (a s)")
                    act.activation(dst, gp[:, 2], ACT.Copy).then_inc(hi_done, 1)

                def unit(pos, j, first):
                    prev = Pos(pos.const - per, pos.step, pos.i)
                    for s in range(per):
                        if s >= 2:
                            C_(pos, s - 2, first and s - 2 < 2)
                        elif not first:
                            C_(prev, per - 2 + s, False)
                        E_(pos, s, first and s < 4)
                        if s == turn and not first:
                            H_(j - 1)
                unit(Pos(t0), 0, True)
                if looped:
                    with act.Fori(1, n) as j:
                        unit(Pos(t0, per, j), j, False)
                else:
                    for j in range(1, n):
                        unit(Pos(t0 + per * j), j, False)
                for s in range(per - 2, per):
                    C_(Pos(t0 + per * (n - 1)), s, False)
                H_(n - 1)

            def head_exp(s):
                w = (s % 4 + 1) * P
                return act.activation(prob[:, s % 4, 0:w], prob[:, s % 4, 0:w], ACT.Exp, scale=-1.0,
                                      bias=nmax[:, s % 4:s % 4 + 1], accum_out=rsum[:, s % 4:s % 4 + 1])
            causal = [P, 2 * P, 3 * P, 4 * P] * 2
            attention(fox, A, 0, 8, 8, True, head_exp, causal)
            add_and_prep(wo, B, "ffn1")
            act.wait_ge(p_ready, 32)
            act.activation(p_hi1[:], p_raw1[:], ACT.Copy).then_inc(hi_done, 1)
            act.wait_ge(sp_chain, 1)
            act.activation(sp[:, 1], sp[:, 0], ACT.Exp, scale=-1.0).then_inc(sp_e, 1)
            ffn_layer(1, B, A)

            for s in range(2):
                next_of(gqx, s)
                if s == 0:
                    act.wait_ge(var_done, fin["norm"] + 1)
                    act.activation(rstd[:], T[:, 1], ACT.Sqrt).then_inc(rstd_done, 1)
                    finish_col(1)
                    act.activation(var[:], var[:], ACT.Sqrt).then_inc(rstd_done, 1)

            def x_exp(s):
                return act.activation(prob[:, s % 4, 0:MEM], ms[:, s % 2, 0:MEM], ACT.Exp,
                                      bias=nmax[:, s % 4:s % 4 + 1], accum_out=rsum[:, s % 4:s % 4 + 1])
            attention(xat, B, 4, 4, 4, False, x_exp, [MEM] * 4)

            def branch(n):
                at = br[n]
                for half in range(2):
                    bp = Pos(at["blk"] + 8 * half)
                    for s in range(3):
                        next_w(Pos(at["slab"] + 3 * half + s), Pos(at["blk"] + 8 * half + 2 * s))
                        if s < 2:
                            for c in range(2 * s, 2 * s + 2):
                                wait_evac(act, bp, c)
                                act.activation(T[:, c], T[:, c], ACT.Sigmoid).then_inc(sg_done, 1)
            branch(2)
            for s in range(4):
                next_of(gxg, s)
            for j in range(4):
                wait_evac(act, Pos(gxg["blk"] + 4), j)
                act.activation(ga[:, j], ga[:, j], ACT.Gelu_apprx_tanh).then_inc(gelu_done, 1)
            def lru_hi(j):
                act.wait_ge(l_y, j + 1)
                act.activation(b_hi[:, j], U[:, 0], ACT.Copy).then_inc(hi_done, 1)

            for j, (at, s) in enumerate(((gqm, 0), (gqm, 1), (gkm, 0), (gkm, 1))):
                next_of(at, s)
                if j:
                    act.wait_ge(l_chain, 7 * j)
                    lru_hi(j - 1)
                for r, b in ((0, "lru_ba"), (1, "lru_bx")):
                    act.wait_ge(l_gate, 2 * j + r + 1)
                    act.activation(T[:, r], ms[:, r], ACT.Sigmoid, bias=col(b, j)).then_inc(l_act, 1)
                act.wait_ge(l_act, 4 * j + 1)
                if j == 0:
                    act.wait_ge(sp_chain, SP_OPS)
                act.activation(T[:, 2], T[:, 0], ACT.Tanh, scale=sp[:, 7, j:j + 1]).then_inc(l_act, 1)
                act.wait_ge(l_act, 4 * j + 3)
                act.activation(T[:, 3], T[:, 2], ACT.Sqrt).then_inc(l_act, 1)
            for s in range(2):
                next_of(gvm, s, 4 * s)
                if s == 0:
                    lru_hi(3)
            branch(0)

            attention(mob, B, 4, 4, 8, True, head_exp, causal)
            branch(1)
            for k in range(8):
                act.wait_ge(gm_done, br[1]["gm"] + 8)
                act.activation(a_hi[:, k], merged[:, k], ACT.Copy).then_inc(hi_done, 1)
            add_and_prep(wout, B, "ffn2")

            f = ffn2

            def gu(sp_, bp, gl, fu, k):
                next_w(sp_, bp)
                if bp.const == f["blk"]:
                    finish_norm(wout)
                act.wait_ge(g_chain, gl.at(3 * (k + 1)))
                i = gl.i
                bias = col("cb", k) if not gl.step else par[:, bass.ds(COL["cb"] + 8 + k + 8 * i, 1)]
                act.activation(T[:, k % 2], T[:, k % 2], ACT.Gelu_apprx_tanh, bias=bias).then_inc(gelu_done, 1)
                act.wait_ge(full, fu.at(k + 1))
                act.activation(a_hi[:, k], U[:, k % 2], ACT.Copy).then_inc(hi_done, 1)
            for k in range(8):
                gu(Pos(f["slab"] + k), Pos(f["blk"] + 2 * k), Pos(0), Pos(f["full"]), k)
            with act.Fori(0, 2) as i:
                for s in range(4):
                    next_w(Pos(f["slab"] + 8 + s, 12, i), Pos(f["blk"] + 16 + 2 * s, 24, i))
                for k in range(8):
                    gu(Pos(f["slab"] + 12 + k, 12, i), Pos(f["blk"] + 24 + 2 * k, 24, i), Pos(24, 24, i), Pos(f["full"] + 8, 8, i), k)
            for s in range(4):
                next_of(f, 32 + s)
                for c in range(2):
                    k = 2 * s + c
                    wait_evac(act, Pos(f["blk"] + 64), k)
                    square(k, f)
            finish_norm(f)

        @block.vector
        def _(v):
            def tt(o, a, b, op):
                return v.tensor_tensor(o, a, b, op)

            def stt(o, a, s, b, op0, op1):
                return v.scalar_tensor_tensor(o, a, s, b, op0, op1)

            def low(at, n, o, full_ap, hi):
                v.wait_ge(hi_done, at + n + 1)
                tt(o, full_ap, f32(hi), ALU.subtract).then_inc(lo_done, 1)

            def low_h(at, k, X, gain):
                v.wait_ge(hi_done, at["split"] + k + 1)
                stt(X[1][:, k], h[:, k], col(gain, k), f32(X[0][:, k]), ALU.mult, ALU.subtract).then_inc(lo_done, 1)

            def add_square(at, k):
                if k == 0:
                    return
                v.wait_ge(sq_done, at["sq"] + k + 1)
                if k >= 2:
                    v.wait_ge(acc_done, at["acc"] + k - 1)
                tt(acc_sq[:], acc_sq[:], sqb[:, k % 2], ALU.add).then_inc(acc_done, 1)

            def prep(at, k, X, gain, soff=0):
                v.wait_ge(hi_done, at["split"] + soff + k + 1)
                stt(X[1][:, k], h[:, k], col(gain, k), f32(X[0][:, k]), ALU.mult, ALU.subtract).then_inc(lo_done, 1)
                add_square(at, k)

            def finish_var(at):
                v.wait_ge(eps_done, at["norm"] + 1)
                v.reciprocal(var[:], var[:]).then_inc(var_done, 1)

            def norm(at):
                v.wait_ge(stat_done, at["stat"] + 1)
                if at["norm"]:
                    v.wait_ge(rstd_done, at["norm"])
                v.tensor_scalar(var[:], ms[:, 0], EPS, None, ALU.add).then_inc(eps_done, 1)
                finish_var(at)

            def norm_col(n):
                v.wait_ge(col_stat, n + 1)
                v.tensor_scalar(colv[:], ms[:, 1, 0:QB], EPS, None, ALU.add).then_inc(col_eps, 1)
                v.wait_ge(col_eps, n + 1)
                v.reciprocal(colv[:], colv[:]).then_inc(col_var, 1)

            def scaled(o, bp, c):
                wait_blk(v, bp, c)
                b = bp.slot(4, c)
                tt(o, gp[:, b], rstd[:], ALU.mult).then_inc(evac[b], 1)

            v.wait_ge(par_ready, 16)
            tt(fin_gain[:], col("final1", 0, KB), col("mix2", 0, KB), ALU.mult).then_inc(fin_gain_done, 1)
            for k in range(8):
                prep(x0, k, A, "mix0")
            norm(x0)
            v.wait_ge(rstd_done, 1)

            v.wait_ge(pad_zero, 1)

            def pair_out(bp):
                for c in range(4):
                    scaled(T[:, c], bp, c)

            def pair_u(bp, i, pcol):
                for s in range(2):
                    v.wait_ge(sg_done, 2 * i + s + 1)
                    wait_evac(v, bp, 2 * s)
                    stt(u_of(2 * i + s, TAPS - 1), T[:, 2 * s], pcol("b_a1", s, 0), T[:, 2 * s + 1], ALU.add, ALU.mult).then_inc(u_done, 1)

            def conv(i, pcol, between=None):
                c0 = CONV_OPS * i
                for n in range(TAPS - POOL_TAPS):
                    for s in range(2):
                        t = POOL_TAPS + n
                        src, sum_ = u_of(2 * i + s, t), ms[:, 3 * s]
                        if n == 0:
                            v.wait_ge(u_done, 2 * i + s + 1)
                            if not isinstance(i, int) or i:
                                v.wait_ge(conv_done, c0)
                            m = v.tensor_scalar(sum_, src, pcol("w_dw", s, 8 * t), None, ALU.mult)
                        else:
                            v.wait_ge(conv_done, c0 + 2 * n + s - 1)
                            m = stt(sum_, src, pcol("w_dw", s, 8 * t), sum_, ALU.mult, ALU.add)
                        m.then_inc(conv_done, 1)
                    if between:
                        between(n)
                for s in range(2):
                    v.wait_ge(conv_done, c0 + CONV_OPS - 3 + s)
                    v.wait_ge(pool_conv, 2 * (POOL_TAPS - 1) * i + 2 * POOL_TAPS - 3 + s)
                    tt(u_of(2 * i + s, TAPS - 1), ms[:, 3 * s], pool_sum[:, s], ALU.add).then_inc(conv_done, 1)

            def colp(i):
                if isinstance(i, int):
                    return lambda n, s, o: col(n, o + s + 2 * i)
                return lambda n, s, o: par[:, bass.ds(COL[n] + o + s + 2 * i, 1)]

            def next_pair(i, n):
                if n == OUT_TAP:
                    v.wait_ge(u_done, 2 * i + 2)
                    pair_out(Pos(4, 4, i))
                if n == U_TAP:
                    pair_u(Pos(4, 4, i), i + 1, lambda nm, s, o: colp(i)(nm, s, o + 2))

            def first_pair(n):
                next_pair(0, n)
                if n == 1:
                    v.wait_ge(mstat_done, 1)
                    v.tensor_scalar(var[:, 0:MEM], ms[:, 1, 0:MEM], EPS, None, ALU.add).then_inc(meps_done, 1)
                if n == 2:
                    v.wait_ge(meps_done, 1)
                    v.reciprocal(var[:, 0:MEM], var[:, 0:MEM]).then_inc(mvar_done, 1)
                if n == 12:
                    v.wait_ge(mrstd_done, 1)
                    for k in range(8):
                        stt(mem_raw[:, k], mem_raw[:, k], col("memg", k), U[:, 0, 0:MEM], ALU.mult, ALU.mult).then_inc(mscaled, 1)
            pair_out(Pos(0))
            pair_u(Pos(0), 0, colp(0))
            conv(0, colp(0), first_pair)
            with v.Fori(1, 3) as i:
                conv(i, colp(i), lambda n: next_pair(i, n))
            conv(3, colp(3))
            v.wait_ge(mean_done, 1)
            for k in range(8):
                tt(big[:, k], big[:, k], ms[:, 1], ALU.subtract).then_inc(centred, 1)
            v.wait_ge(cvar_done, 8)
            v.tensor_scalar(var[:], ms[:, 2], EPS, None, ALU.add).then_inc(eps_done, 1)
            finish_var(ln)
            v.wait_ge(rstd_done, ln["norm"] + 1)
            for k in range(9):
                if k < 8:
                    tt(big[:, k], big[:, k], rstd[:], ALU.mult).then_inc(normed, 1)
                if k >= 1:
                    low(ln["split"], k - 1, b_lo[:, k - 1], U[:, (k - 1) % 2], b_hi[:, k - 1])
            for k in range(9):
                if k < 8:
                    bp = Pos(pw2["blk"])
                    wait_blk(v, bp, k)
                    stt(h[:, k], gp[:, bp.slot(4, k)], col("b_pw2", k), h[:, k], ALU.add, ALU.add).then_inc(evac[bp.slot(4, k)], 1)
                if k >= 1:
                    prep(pw2, k - 1, A, "ffn0")

            def up_block(bp, c, spl, H_, k):
                scaled(T[:, k % 4], bp, c)
                wait_evac(v, bp, c)
                stt(U[:, k % 2], T[:, k % 4], 0.0, T[:, k % 4], ALU.max, ALU.mult).then_inc(full, 1)
                if k >= 1:
                    low_hid(spl, H_, k - 1)

            def low_hid(spl, H_, k):
                v.wait_ge(hi_done, spl.at(k + 1))
                tt(H_[1][:, k], U[:, k % 2], f32(H_[0][:, k]), ALU.subtract).then_inc(lo_done, 1)

            def add_h(bp, k):
                wait_blk(v, bp, k)
                b = bp.slot(4, k)
                tt(h[:, k], gp[:, b], h[:, k], ALU.add).then_inc(evac[b], 1)

            def ffn_layer(l, X, H_):
                f = ffn[l]
                n = pw2 if l == 0 else wo
                norm(n)
                v.wait_ge(rstd_done, n["norm"] + 1)
                for k in range(8):
                    up_block(Pos(f["blk"]), k, Pos(f["split"]), H_, k)
                low_hid(Pos(f["split"]), H_, 7)
                with v.Fori(0, 3) as i:
                    for k in range(8):
                        add_h(Pos(f["blk"] + 8, 16, i), k)
                    for k in range(8):
                        up_block(Pos(f["blk"] + 16, 16, i), k, Pos(f["split"] + 8, 8, i), H_, k)
                    low_hid(Pos(f["split"] + 8, 8, i), H_, 7)
                for k in range(9):
                    if k < 8:
                        add_h(Pos(f["blk"] + 56), k)
                    if k >= 1:
                        prep(f, k - 1, X, "ple%d" % l, soff=32)
                g = gate[l]
                norm(f)
                v.wait_ge(rstd_done, f["norm"] + 1)
                bp = Pos(g["blk"])
                scaled(T[:, 0], bp, 0)
                for c in range(9):
                    if c < 7:
                        scaled(T[:, (c + 1) % 2], bp, c + 1)
                    if c < 8:
                        v.wait_ge(sg_done, g["sg"] + c + 1)
                        tt(T[:, 2 + c % 2], T[:, c % 2], bigs[l][:, c], ALU.mult).then_inc(gm_done, 1)
                        v.wait_ge(gm_done, g["gm"] + c + 1)
                        tt(h[:, c], h[:, c], T[:, 2 + c % 2], ALU.add).then_inc(hg_done, 1)
                    if c >= 1:
                        if l == 0:
                            prep(g, c - 1, B, "mix1")
                        else:
                            add_square(g, c - 1)
                            k = c - 1
                            v.wait_ge(hi_done, fin["split"] + k + 1)
                            stt(a_lo[:, k], h[:, k], fin_gain[:, k:k + 1], f32(a_hi[:, k]), ALU.mult, ALU.subtract).then_inc(lo_done, 1)
                            if k >= 1:
                                v.wait_ge(fin_sq, k + 1)
                                if k >= 2:
                                    v.wait_ge(fin_acc, k - 1)
                                tt(acc_fin, acc_fin, U[:, k % 2], ALU.add).then_inc(fin_acc, 1)
            ffn_layer(0, A, B)

            norm(gate[0])
            norm_col(0)
            v.wait_ge(rstd_done, gate[0]["norm"] + 1)
            for k in range(8):
                bp = Pos(gq["blk"])
                wait_blk(v, bp, k)
                b = bp.slot(4, k)
                stt(qT[:, k], gp[:, b], 0.125, rstd[:], ALU.mult, ALU.mult).then_inc(evac[b], 1)
                for n in range(2 * k - 2, min(2 * k, 8)):
                    if n >= 0:
                        low_h(kvsplit, n, A, "kv")
                if k == 5:
                    v.wait_ge(wf_hi_done, 1)
                    tt(wf_lo[:, :, 0:16], wf[:], f32(wf_hi[:, :, 0:16]), ALU.subtract).then_inc(wf_split, 1)

            def v_blocks(at, dst, n):
                for s in range(n):
                    for t in range(QB):
                        bp = Pos(at["blk"] + 4 * s)
                        wait_blk(v, bp, t)
                        b = bp.slot(4, t)
                        v.tensor_scalar(dst[:, t, 256 * s:256 * s + 256], gp[:, b, 0:256], rcol[:, t:t + 1], None,
                                        ALU.mult).then_inc(evac[b], 1)
            R = slice(0, 16)
            f_, ax, e, z, z2, pl = T[R, 0], T[R, 1], T[R, 2], T[R, 3], U[R, 0], U[R, 1]
            chain = [0]

            def link(ins):
                chain[0] += 1
                ins.then_inc(f_chain, 1)
                v.wait_ge(f_chain, chain[0])

            def log1p_z(e, z, z2, rd, lk):
                lk(v.tensor_scalar(z2, e, 2.0, None, ALU.add))
                lk(v.reciprocal(rd, z2))
                lk(tt(z, e, rd, ALU.mult))
                lk(tt(z2, z, z, ALU.mult))

            def log1p_series(z, z2, pl, lk):
                lk(v.tensor_scalar(pl, z2, ATANH[-1], None, ALU.mult))
                for cf in ATANH[-2::-1]:
                    lk(stt(pl, pl, cf, z2, ALU.add, ALU.mult))
                lk(stt(pl, pl, 1.0, z, ALU.add, ALU.mult))

            for k in range(8):
                scaled(kT[:, k], Pos(gk["blk"]), k)
                if k == 0:
                    v.wait_ge(f_stat, 1)
                    link(tt(f_, ms[R, 2], rstd[R], ALU.mult))
                    v.tensor_scalar(f_, f_, par[R, COL["b_f"]:COL["b_f"] + 1], None, ALU.add).then_inc(f_v, 1)
                    v.wait_ge(f_v, 1)
                    stt(ax, f_, -1.0, f_, ALU.mult, ALU.max).then_inc(f_v, 1)
                if k == 1:
                    v.wait_ge(f_exp, 1)
                    log1p_z(e, z, z2, ax, link)
                if k == 3:
                    log1p_series(z, z2, pl, link)
                if k == 5:
                    link(v.tensor_scalar(f_, f_, 0.0, None, ALU.min))
                    link(stt(pl, pl, 2.0, f_, ALU.mult, ALU.subtract))
                    link(v.memset(z2, 1.0))
                    v.tensor_tensor_scan(z, z2, pl, 0.0, ALU.mult, ALU.add).then_inc(f_v, 1)
            v.wait_ge(col_done, 1)
            v_blocks(gv, v_s, 4)

            def attention(at, X, k0, n, per, looped, bias, ow, qb_of, col_of):
                t0, turn = at["step"], min(TURN, per - 1)

                def B_(pos, j, s, fresh):
                    v.wait_ge(scored, pos.at(s + 1))
                    if not fresh:
                        v.wait_ge(transposed, pos.at(s - 3))
                    bias(j, s).then_inc(biased, 1)

                def N_(pos, j, s):
                    if s == 0 and not (isinstance(j, int) and j == 0):
                        v.wait_ge(ot_done, at["unit"] + j)
                    v.wait_ge(exped, pos.at(s + 1))
                    v.reciprocal(rinv[:, s % 4:s % 4 + 1], rsum[:, s % 4:s % 4 + 1]).then_inc(sum_inv, 1)
                    v.wait_ge(sum_inv, pos.at(s + 1))
                    v.wait_ge(pv_done, pos.at(s + 1))
                    c0 = col_of(s)
                    v.tensor_scalar(o_sb[:, qb_of(s), c0:c0 + ow], gp[:, s % 2, 0:ow], rinv[:, s % 4:s % 4 + 1], None,
                                    ALU.mult).then_inc(o_done, 1)

                def L_(j):
                    v.wait_ge(hi_done, at["split"] + j + 1)
                    at_ = (lambda t: t[:, k0 + j]) if isinstance(j, int) else (
                        lambda t: t[:, bass.ds(k0 + j, 1)].rearrange("p a s -> p (a s)"))
                    tt(at_(X[1]), gp[:, 2], f32(at_(X[0])), ALU.subtract).then_inc(lo_done, 1)

                def unit(pos, j, first):
                    prev = Pos(pos.const - per, pos.step, pos.i)
                    for s in range(per):
                        B_(pos, j, s, first and s < 4)
                        if s >= 4:
                            N_(pos, j, s - 4)
                        elif not first:
                            N_(prev, j - 1, per - 4 + s)
                        if s == min(turn + 1, per - 1) and not first:
                            L_(j - 1)
                unit(Pos(t0), 0, True)
                if looped:
                    with v.Fori(1, n) as j:
                        unit(Pos(t0, per, j), j, False)
                else:
                    for j in range(1, n):
                        unit(Pos(t0 + per * j), j, False)
                for s in range(per - 4, per):
                    N_(Pos(t0 + per * (n - 1)), n - 1, s)
                L_(n - 1)

            def head_bias(b_of, ready):
                def bias(j, s):
                    hh, qb = s // 4, s % 4
                    if qb == 0:
                        ready(j, hh)
                    w = (qb + 1) * P
                    v.sem_inc(step_open, 1)
                    return v.tensor_tensor_reduce(prob[:, s % 4, 0:w], ms[:, s % 2, 0:w], b_of(hh, qb, w), -1.0, 3e38,
                                                  ALU.add, ALU.min, nmax[:, s % 4:s % 4 + 1])
                return bias
            attention(fox, A, 0, 8, 8, True,
                      head_bias(lambda hh, qb, w: fbias[:, hh, 0:w], lambda j, hh: v.wait_ge(bias_ready[hh], 16 * (j + 1))),
                      64, lambda s: s % 4, lambda s: 64 * (s // 4))
            for k in range(9):
                if k < 8:
                    add_h(Pos(wo["blk"]), k)
                if k >= 1:
                    prep(wo, k - 1, B, "ffn1")
            low(p_split[1]["split"], 0, p_lo1[:], p_raw1[:], p_hi1[:])
            chain_sp = [0]

            def link_sp(ins):
                chain_sp[0] += 1
                ins.then_inc(sp_chain, 1)
                v.wait_ge(sp_chain, chain_sp[0])
            lam = par[:, COL["lam"]:COL["lam"] + 4]
            link_sp(stt(sp[:, 0], lam, -1.0, lam, ALU.mult, ALU.max))
            v.wait_ge(sp_e, 1)
            log1p_z(sp[:, 1], sp[:, 2], sp[:, 3], sp[:, 5], link_sp)
            log1p_series(sp[:, 2], sp[:, 3], sp[:, 4], link_sp)
            link_sp(v.tensor_scalar(sp[:, 6], lam, -1.0, 0.0, ALU.mult, ALU.max))
            link_sp(stt(sp[:, 6], sp[:, 4], 2.0, sp[:, 6], ALU.mult, ALU.add))
            link_sp(v.tensor_scalar(sp[:, 7], sp[:, 6], 4.0, None, ALU.mult))
            assert chain_sp[0] == SP_OPS
            ffn_layer(1, B, A)

            v.wait_ge(stat_done, fin["stat"] + 1)
            v.wait_ge(rstd_done, gate[1]["norm"])
            v.tensor_scalar(var[:], ms[:, 0], EPS, None, ALU.add).then_inc(eps_done, 1)
            finish_var(gate[1])
            v.wait_ge(var_done, gate[1]["norm"] + 1)
            tt(T[:, 1], ms[:, 2], var[:], ALU.mult).then_inc(fin_chain, 1)
            v.wait_ge(fin_chain, 1)
            v.tensor_scalar(T[:, 1], T[:, 1], EPS, None, ALU.add).then_inc(eps_done, 1)
            v.wait_ge(eps_done, fin["norm"] + 1)
            v.reciprocal(T[:, 1], T[:, 1]).then_inc(fin_chain, 1)
            v.wait_ge(fin_chain, 2)
            tt(T[:, 1], T[:, 1], var[:], ALU.mult).then_inc(var_done, 1)
            v.wait_ge(col_stat, 2)
            v.tensor_scalar(colv[:], ms[:, 1, 0:QB], EPS, None, ALU.add).then_inc(col_eps, 1)
            v.wait_ge(col_eps, 2)
            v.reciprocal(colv[:], colv[:]).then_inc(fin_chain, 1)
            v.wait_ge(fin_chain, 3)
            tt(colv2[:], ms[:, 1, QB:2 * QB], colv[:], ALU.mult).then_inc(fin_chain, 1)
            v.wait_ge(fin_chain, 4)
            v.tensor_scalar(colv2[:], colv2[:], EPS, None, ALU.add).then_inc(fin_chain, 1)
            v.wait_ge(fin_chain, 5)
            v.reciprocal(colv2[:], colv2[:]).then_inc(fin_chain, 1)
            v.wait_ge(fin_chain, 6)
            tt(colv[:], colv[:], colv2[:], ALU.mult).then_inc(col_var, 1)
            v.wait_ge(rstd_done, fin["norm"])
            for k in range(4):
                bp = Pos(gqx["blk"])
                wait_blk(v, bp, k)
                stt(qx[:, k], gp[:, bp.slot(4, k)], float(P) ** -0.5, rstd[:], ALU.mult, ALU.mult).then_inc(evac[bp.slot(4, k)], 1)

            def x_max(j, s):
                return v.tensor_reduce(nmax[:, s % 4:s % 4 + 1], ms[:, s % 2, 0:MEM], AX.X, ALU.max, negate=True)
            attention(xat, B, 4, 4, 4, False, x_max, P, lambda s: s, lambda s: 0)

            def branch(n, last=False):
                at = br[n]
                for half in range(2):
                    bp = Pos(at["blk"] + 8 * half)
                    if n != 2 and half:
                        v.wait_ge(gm_done, at["gm"] + 4)
                    for c in range(4):
                        scaled(T[:, c], bp, c)
                    for c in range(4):
                        v.wait_ge(sg_done, at["sg"] + 4 * half + c + 1)
                        wait_blk(v, bp, 4 + c)
                        b, m = bp.slot(4, 4 + c), merged[:, 4 * half + c]
                        if n == 2:
                            tt(m, gp[:, b], T[:, c], ALU.mult).then_inc(evac[b], 1)
                        else:
                            tt(T[:, c], gp[:, b], T[:, c], ALU.mult).then_inc(evac[b], 1)
                            wait_evac(v, bp, 4 + c)
                            tt(m, m, T[:, c], ALU.add).then_inc(gm_done, 1)
            v.wait_ge(lo_done, fin["split"] + 8)
            v.wait_ge(rstd_done, fin["norm"] + 1)
            for n in range(KB):
                stt(h[:, n], h[:, n], col("final1", n), var[:], ALU.mult, ALU.mult).then_inc(h_done, 1)
            branch(2)
            v.wait_ge(pad_zero, 2)
            for j in range(4):
                scaled(xap[:, j, 3:], Pos(gxg["blk"]), j)
            for j in range(4):
                scaled(ga[:, j], Pos(gxg["blk"] + 4), j)
                for t in range(4):
                    src = xap[:, j, t:t + S]
                    if t == 0:
                        wait_evac(v, Pos(gxg["blk"]), j)
                        m = v.tensor_scalar(xc[:, j], src, col("lru_w", j), col("lru_b", j), ALU.mult, ALU.add)
                    else:
                        v.wait_ge(xa_c, 4 * j + t)
                        m = stt(xc[:, j], src, col("lru_w", 4 * t + j), xc[:, j], ALU.mult, ALU.add)
                    m.then_inc(xa_c, 1)
            lch = [0]

            def link_l(ins):
                lch[0] += 1
                ins.then_inc(l_chain, 1)
                v.wait_ge(l_chain, lch[0])
            for j in range(4):
                v.wait_ge(l_act, 4 * j + 3)
                if j:
                    v.wait_ge(lo_done, lru["split"] + j)
                link_l(v.tensor_scalar(U[:, 0], T[:, 2], 1.0, None, ALU.add))
                link_l(v.reciprocal(U[:, 0], U[:, 0]))
                link_l(v.tensor_scalar(T[:, 0], U[:, 0], 2.0, -1.0, ALU.mult, ALU.add))
                v.wait_ge(l_act, 4 * j + 4)
                link_l(tt(T[:, 3], T[:, 3], U[:, 0], ALU.mult))
                link_l(stt(T[:, 3], T[:, 3], 2.0, T[:, 1], ALU.mult, ALU.mult))
                link_l(tt(T[:, 3], T[:, 3], xc[:, j], ALU.mult))
                link_l(v.tensor_tensor_scan(U[:, 1], T[:, 0], T[:, 3], 0.0, ALU.mult, ALU.add))
                v.wait_ge(gelu_done, j + 1)
                tt(U[:, 0], U[:, 1], ga[:, j], ALU.mult).then_inc(l_y, 1)
                if j == 0:
                    v.wait_ge(xa_c, 16)
                for k in range(2 * (j % 2), 2 * (j % 2) + 2):
                    if j < 2:
                        bp = Pos(gqm["blk"])
                        wait_blk(v, bp, k)
                        b = bp.slot(4, k)
                        stt(qm[:, k], gp[:, b], 0.125, rstd[:], ALU.mult, ALU.mult).then_inc(evac[b], 1)
                    else:
                        scaled(km[:, k], Pos(gkm["blk"]), k)
                low(lru["split"], j, b_lo[:, j], U[:, 0], b_hi[:, j])
            v.wait_ge(lo_done, lru["split"] + 4)
            v.wait_ge(col_done, 2)
            v_blocks(gvm, vm, 2)
            branch(0)
            attention(mob, B, 4, 4, 8, True,
                      head_bias(lambda hh, qb, w: mbias[:, hh, 3 * P - qb * P:3 * P - qb * P + w],
                                lambda j, hh: v.wait_ge(mb_ready, 2 * j + hh + 1)),
                      64, lambda s: s % 4, lambda s: 64 * (s // 4))
            branch(1)
            for k in range(8):
                low(mrg["split"], k, a_lo[:, k], merged[:, k], a_hi[:, k])
            v.wait_ge(h_done, 8)
            for k in range(9):
                if k < 8:
                    add_h(Pos(wout["blk"]), k)
                if k >= 1:
                    prep(wout, k - 1, B, "ffn2")

            f = ffn2
            norm(wout)
            v.wait_ge(rstd_done, wout["norm"] + 1)
            v.wait_ge(pad_zero, 3)

            def gu(bp, gl, ge, spl, k, w_of):
                g = k % 2
                scaled(gpad[:, g, 2:], bp, 2 * k)
                wait_evac(v, bp, 2 * k)
                v.tensor_scalar(T[:, g], gpad[:, g, 0:S], w_of(k, 0), None, ALU.mult).then_inc(g_chain, 1)
                for t in range(1, 3):
                    v.wait_ge(g_chain, gl.at(3 * k + t))
                    stt(T[:, g], gpad[:, g, t:t + S], w_of(k, t), T[:, g], ALU.mult, ALU.add).then_inc(g_chain, 1)
                scaled(T[:, 2 + g], bp, 2 * k + 1)
                v.wait_ge(gelu_done, ge.at(k + 1))
                wait_evac(v, bp, 2 * k + 1)
                tt(U[:, g], T[:, 2 + g], T[:, g], ALU.mult).then_inc(full, 1)
                if k >= 1:
                    low_hid(spl, A, k - 1)
                if k == 7:
                    low_hid(spl, A, 7)
            for k in range(8):
                gu(Pos(f["blk"]), Pos(0), Pos(4), Pos(f["split"]), k, lambda k, t: col("cw", 24 * t + k))
            with v.Fori(0, 2) as i:
                for k in range(8):
                    add_h(Pos(f["blk"] + 16, 24, i), k)
                for k in range(8):
                    gu(Pos(f["blk"] + 24, 24, i), Pos(24, 24, i), Pos(12, 8, i), Pos(f["split"] + 8, 8, i), k,
                       lambda k, t: par[:, bass.ds(COL["cw"] + 24 * t + 8 + k + 8 * i, 1)])
            for k in range(9):
                if k < 8:
                    add_h(Pos(f["blk"] + 64), k)
                if k >= 1:
                    add_square(f, k - 1)
            norm(f)
            v.wait_ge(rstd_done, f["norm"] + 1)
            for k in range(8):
                stt(h[:, k], h[:, k], col("final2", k), rstd[:], ALU.mult, ALU.mult).then_inc(out_ready, 1)


def _tiles(w, rows, cols):
    import numpy as np
    w = np.concatenate([w[:, c:c + P] for c in cols], axis=1)
    return w.reshape(rows, P, len(cols) * P).transpose(1, 0, 2).reshape(P, SLAB)


def _slabs(i):
    import numpy as np
    out = []

    def plain(w, c0=0, c1=None, rows=8):
        per = 16 // rows
        c1 = w.shape[1] if c1 is None else c1
        for c in range(c0, c1, per * P):
            out.append(_tiles(w, rows, [c + P * n for n in range(per)]))

    def pairs(w0, w1, cols0, cols1):
        for a, b in zip(cols0, cols1):
            out.append(np.concatenate([w0[:, a:a + P], w1[:, b:b + P]], axis=1)
                       .reshape(8, P, 2 * P).transpose(1, 0, 2).reshape(P, SLAB))

    pw1 = i["conv_w_pw1"][0]
    pairs(pw1, pw1, range(0, D, P), range(D, 2 * D, P))
    plain(i["w_mem_kv_2"][0])
    plain(i["conv_w_pw2"][0])

    def ffn(l):
        for c in range(4):
            plain(i["ffn_w1"][l], c * D, (c + 1) * D)
            plain(i["ffn_w2"][l][c * D:(c + 1) * D])
        plain(i["ple_w_proj"][l], rows=2)
        plain(i["ple_w_gate"][l])
    ffn(0)
    plain(i["attn_w_q"][0])
    plain(i["w_kvf"], 0, 2 * D)
    plain(i["attn_w_o"][0])
    ffn(1)
    w = i["w_in_2"][0]
    plain(w, 5 * HALF, 6 * HALF)

    def branch(n):
        for half in range(2):
            c = 6 * HALF + n * D + half * HALF
            plain(w, c, c + HALF)
            plain(i["w_branch_2"][0, n], half * HALF, (half + 1) * HALF, rows=4)
    branch(2)
    plain(w, 0, 2 * HALF)
    plain(w, 2 * HALF, 5 * HALF)
    branch(0)
    branch(1)
    plain(i["w_out_2"][0])
    for c in range(3):
        pairs(i["w_ffn_gate_2"][0], i["w_ffn_up_2"][0], range(c * D, (c + 1) * D, P), range(c * D, (c + 1) * D, P))
        plain(i["w_ffn_down_2"][0][c * D:(c + 1) * D])
    return np.stack(out)


def _params(i):
    import numpy as np

    def cols(*vs):
        return np.concatenate([np.asarray(v).reshape(-1, P).T for v in vs], axis=1)
    b1 = i["conv_b_pw1"][0]
    slope = np.broadcast_to((2.0 ** -np.arange(1.0, 9.0)).astype(np.float32), (P, 8))
    b_f = np.zeros((P, 1), np.float32)
    b_f[0:16, 0] = i["b_f"]
    parts = {
        "mix0": cols(i["mix_norm"][0]), "mix1": cols(i["mix_norm"][1]), "b_a1": cols(b1[:D]), "b_g1": cols(b1[D:]),
        "w_dw": cols(*i["conv_w_dw"][0]), "b_dw": cols(i["conv_b_dw"][0]), "ln_g": cols(i["conv_ln_g"][0]),
        "ln_b": cols(i["conv_ln_b"][0]), "b_pw2": cols(i["conv_b_pw2"][0]), "kv": cols(i["kv_norm"]),
        "ffn0": cols(i["ffn_norm"][0]), "ffn1": cols(i["ffn_norm"][1]), "ple0": cols(i["ple_norm"][0]),
        "ple1": cols(i["ple_norm"][1]), "final1": cols(i["final_norm"]), "mix2": cols(i["mix_norm_gain_2"][0]),
        "lru_w": cols(*i["lru_conv_w_2"][0]), "lru_b": cols(i["lru_conv_b_2"][0]),
        "lru_ba": cols(i["lru_b_a_2"][0].reshape(-1)), "lru_bx": cols(i["lru_b_x_2"][0].reshape(-1)),
        "lam": cols(i["lru_lambda_2"][0]), "memg": cols(i["mem_norm_gain_2"][0]), "ffn2": cols(i["ffn_norm_gain_2"][0]),
        "cw": cols(*i["ffn_conv_w_2"][0]), "cb": cols(i["ffn_conv_b_2"][0]), "final2": cols(i["final_norm_gain_2"]),
        "slope": slope, "b_f": b_f,
    }
    return np.concatenate([parts[n] for n, _ in PARAM_BLOCKS], axis=1)


def _major(a):
    return a.reshape(a.shape[0], -1, P).transpose(2, 1, 0)


def kernel(**inputs):
    import numpy as np
    import concourse.bacc as bacc
    from concourse.bass_utils import run_bass_kernel_spmd

    i = {k: np.asarray(v) for k, v in inputs.items()}
    arrays = {
        "w": _slabs(i), "par": _params(i), "x": _major(i["x"][0]), "mem": _major(i["mem_2"][0]),
        "p": np.stack([_major(i["p"][l, 0]) for l in range(2)]),
        "wf": i["w_kvf"][:, 2 * D:].reshape(KB, P, 16).transpose(1, 0, 2),
        "w_a": i["lru_w_a_2"][0].reshape(4, 2, 64, 64), "w_x": i["lru_w_x_2"][0].reshape(4, 2, 64, 64),
    }
    arrays = {k: np.ascontiguousarray(a) for k, a in arrays.items()}
    nc = bacc.Bacc("TRN2", target_bir_lowering=False, num_devices=1)
    hbm = {k: nc.dram_tensor(k + "_hbm", a.shape, mybir.dt.from_np(a.dtype), kind="ExternalInput").ap()
           for k, a in arrays.items()}
    out = nc.dram_tensor("out_hbm", (P, KB, S), F32, kind="ExternalOutput").ap()
    build(nc, hbm, out)
    r = run_bass_kernel_spmd(nc, [{k + "_hbm": a for k, a in arrays.items()}], core_ids=[0])
    got = r.results[0]["out_hbm"]
    return np.ascontiguousarray(got.transpose(2, 1, 0).reshape(1, S, D))
```
